# Optimizing a Trainium2 kernel written in Bass

```python
import jax, jax.numpy as jnp
from jax import lax
import numpy as np

D_MODEL = 1024
BATCH = 1
SEQ = 512
DEPTH = 2

POOL_WINDOWS = (2, 4, 8, 16)
POOL_GROUPS = len(POOL_WINDOWS)
POOL_GROUP_DIM = D_MODEL // 8
POOL_DIM = POOL_GROUPS * POOL_GROUP_DIM
POOL_WMAX = max(POOL_WINDOWS)
HEAD_DIM = 64
N_Q_HEADS = D_MODEL // 128
N_KV_HEADS = 2
GQA_GROUP = N_Q_HEADS // N_KV_HEADS
ATTN_DIM = N_Q_HEADS * HEAD_DIM
KV_DIM = N_KV_HEADS * HEAD_DIM
WINDOW = 128
BLOCK = 128
ROPE_THETA = 500000.0
ROT_DIM = HEAD_DIM // 4
N_BRANCHES = 2
IN_DIM = POOL_DIM + ATTN_DIM + 2 * KV_DIM + N_BRANCHES * D_MODEL
D_FF = 2816
EPS = 1e-6


def rmsnorm(x, g):
    xf = x.astype(jnp.float32)
    y = xf * lax.rsqrt(jnp.mean(xf * xf, axis=-1, keepdims=True) + EPS)
    return (y * g.astype(jnp.float32)).astype(x.dtype)

def swiglu(h, w_gu, w_down):
    g, u = jnp.split(h @ w_gu, 2, axis=-1)
    return (jax.nn.silu(g) * u) @ w_down

def pool_mixer(u, w_grp, scale):
    B, S, _ = u.shape
    uf = u.astype(jnp.float32)
    c = jnp.cumsum(uf, axis=1)
    c_pad = jnp.pad(c, ((0, 0), (POOL_WMAX, 0), (0, 0)))
    t = jnp.arange(S)
    outs = []
    for g, w in enumerate(POOL_WINDOWS):
        lo, hi = g * POOL_GROUP_DIM, (g + 1) * POOL_GROUP_DIM
        win_sum = c[:, :, lo:hi] - c_pad[:, POOL_WMAX - w:POOL_WMAX - w + S, lo:hi]
        count = jnp.minimum(t + 1, w).astype(jnp.float32)[None, :, None]
        outs.append(win_sum / count - uf[:, :, lo:hi])
    d = jnp.stack(outs, axis=2).astype(u.dtype)
    y = jnp.einsum('bsgc,gcd->bsgd', d, w_grp).reshape(B, S, POOL_DIM)
    return y * scale

def partial_rope(x, cos, sin):
    half = ROT_DIM // 2
    x1 = x[..., :half].astype(jnp.float32)
    x2 = x[..., half:ROT_DIM].astype(jnp.float32)
    c = cos[None, :, None, :]
    s = sin[None, :, None, :]
    rot = jnp.concatenate([x1 * c - x2 * s, x2 * c + x1 * s], axis=-1).astype(x.dtype)
    return jnp.concatenate([rot, x[..., ROT_DIM:]], axis=-1)

def swa_sink_attention(q, k, v, sinks):
    B, S = q.shape[0], q.shape[1]
    nb = S // BLOCK
    qb = q.reshape(B, nb, BLOCK, N_KV_HEADS, GQA_GROUP, HEAD_DIM)

    def with_prev(t):
        tb = t.reshape(B, nb, BLOCK, N_KV_HEADS, HEAD_DIM)
        prev = jnp.pad(tb[:, :-1], ((0, 0), (1, 0), (0, 0), (0, 0), (0, 0)))
        return jnp.concatenate([prev, tb], axis=2)

    kb, vb = with_prev(k), with_prev(v)
    s = jnp.einsum('bnqhgd,bnkhd->bnhgqk', qb, kb).astype(jnp.float32) * (HEAD_DIM ** -0.5)
    qi = jnp.arange(BLOCK)[:, None]
    ki = jnp.arange(2 * BLOCK)[None, :]
    diff = qi + BLOCK - ki
    band = (diff >= 0) & (diff < WINDOW)
    valid = (jnp.arange(nb)[:, None, None] > 0) | (ki[None] >= BLOCK)
    mask = band[None] & valid
    s = jnp.where(mask[None, :, None, None], s, -jnp.inf)
    sink = sinks.astype(jnp.float32).reshape(1, 1, N_KV_HEADS, GQA_GROUP, 1, 1)
    m = jnp.maximum(jnp.max(s, axis=-1, keepdims=True), sink)
    p = jnp.exp(s - m)
    denom = jnp.sum(p, axis=-1, keepdims=True) + jnp.exp(sink - m)
    p = (p / denom).astype(v.dtype)
    o = jnp.einsum('bnhgqk,bnkhd->bnqhgd', p, vb)
    return o.reshape(B, S, ATTN_DIM)

def first_inputs(seed: int = 0) -> dict:
    key = jax.random.key(seed)
    ks = jax.random.split(key, 17)
    f32 = jnp.float32

    def w(k, shape, fan_in):
        return jax.random.normal(k, shape, f32) * (fan_in ** -0.5)

    def gain(k, shape):
        return 1.0 + 0.05 * jax.random.normal(k, shape, f32)

    L = DEPTH
    return {
        "x": jax.random.normal(ks[0], (BATCH, SEQ, D_MODEL), f32),
        "ln_ffn1": gain(ks[1], (L, D_MODEL)),
        "w_ffn1_gu": w(ks[2], (L, D_MODEL, 2 * D_FF), D_MODEL),
        "w_ffn1_down": w(ks[3], (L, D_FF, D_MODEL), D_FF),
        "ln_mix": gain(ks[4], (L, D_MODEL)),
        "w_in": w(ks[5], (L, D_MODEL, IN_DIM), D_MODEL),
        "pool_w": w(ks[6], (L, POOL_GROUPS, POOL_GROUP_DIM, POOL_GROUP_DIM), POOL_GROUP_DIM),
        "pool_scale": 1.0 + 0.1 * jax.random.normal(ks[7], (L, POOL_DIM), f32),
        "w_pool_branch": w(ks[8], (L, POOL_DIM, D_MODEL), POOL_DIM),
        "q_norm": gain(ks[9], (L, HEAD_DIM)),
        "k_norm": gain(ks[10], (L, HEAD_DIM)),
        "sinks": 0.5 * jax.random.normal(ks[11], (L, N_Q_HEADS), f32),
        "w_attn_branch": w(ks[12], (L, ATTN_DIM, D_MODEL), ATTN_DIM),
        "w_out": w(ks[13], (L, D_MODEL, D_MODEL), D_MODEL),
        "ln_ffn2": gain(ks[14], (L, D_MODEL)),
        "w_ffn2_gu": w(ks[15], (L, D_MODEL, 2 * D_FF), D_MODEL),
        "w_ffn2_down": w(ks[16], (L, D_FF, D_MODEL), D_FF),
    }

def first_block(x, ln_ffn1, w_ffn1_gu, w_ffn1_down, ln_mix, w_in, pool_w, pool_scale,
              w_pool_branch, q_norm, k_norm, sinks, w_attn_branch, w_out,
              ln_ffn2, w_ffn2_gu, w_ffn2_down):
    B, S, _ = x.shape
    pos = jnp.arange(S, dtype=jnp.float32)
    inv_freq = ROPE_THETA ** (-jnp.arange(0, ROT_DIM, 2, dtype=jnp.float32) / ROT_DIM)
    ang = pos[:, None] * inv_freq[None, :]
    cos, sin = jnp.cos(ang), jnp.sin(ang)
    splits = [POOL_DIM, POOL_DIM + ATTN_DIM, POOL_DIM + ATTN_DIM + KV_DIM,
              POOL_DIM + ATTN_DIM + 2 * KV_DIM]

    for l in range(DEPTH):
        x = x + 0.5 * swiglu(rmsnorm(x, ln_ffn1[l]), w_ffn1_gu[l], w_ffn1_down[l])

        h = rmsnorm(x, ln_mix[l])
        z = h @ w_in[l]
        u_pool, q, k, v, gate_logits = jnp.split(z, splits, axis=-1)

        a = pool_mixer(u_pool, pool_w[l], pool_scale[l]) @ w_pool_branch[l]

        q = rmsnorm(q.reshape(B, S, N_Q_HEADS, HEAD_DIM), q_norm[l])
        k = rmsnorm(k.reshape(B, S, N_KV_HEADS, HEAD_DIM), k_norm[l])
        v = v.reshape(B, S, N_KV_HEADS, HEAD_DIM)
        q = partial_rope(q, cos, sin)
        k = partial_rope(k, cos, sin)
        b = swa_sink_attention(q, k, v, sinks[l]) @ w_attn_branch[l]

        g_pool, g_attn = jnp.split(jax.nn.sigmoid(gate_logits), N_BRANCHES, axis=-1)
        x = x + (g_pool * a + g_attn * b) @ w_out[l]

        x = x + 0.5 * swiglu(rmsnorm(x, ln_ffn2[l]), w_ffn2_gu[l], w_ffn2_down[l])
    return x


DEPTH_2 = 1

D_MIX = D_MODEL
GDN_HEADS = 4
GDN_DK = 128
GDN_DV = 128
MLSTM_HEADS = 4
MLSTM_DK = 128
MLSTM_DV = 128
N_DIR = 2
CONV_K = 5
CHUNK = 64
PEER_HEADS = 8
PEER_NKEYS = 128
PEER_N = PEER_NKEYS * PEER_NKEYS
PEER_DKEY = 256
PEER_TOPK = 16
PEER_BLOCK = 128

GDN_QK = GDN_HEADS * GDN_DK
GDN_V = GDN_HEADS * GDN_DV
ML_QK = MLSTM_HEADS * MLSTM_DK
ML_V = MLSTM_HEADS * MLSTM_DV
SPLIT_SIZES = (GDN_QK, GDN_QK, GDN_V, GDN_V, N_DIR * GDN_HEADS, N_DIR * GDN_HEADS,
               ML_QK, ML_QK, ML_V, ML_V, N_DIR * MLSTM_HEADS, N_DIR * MLSTM_HEADS)
D_IN = sum(SPLIT_SIZES)


def _rmsnorm(x, g):
    x32 = x.astype(jnp.float32)
    y = x32 * lax.rsqrt(jnp.mean(x32 * x32, axis=-1, keepdims=True) + EPS)
    return (y * g.astype(jnp.float32)).astype(x.dtype)

def _l2norm(x):
    return x * lax.rsqrt(jnp.sum(x * x, axis=-1, keepdims=True) + EPS)

def _to_heads(x, n_heads):
    b, s, _ = x.shape
    return x.astype(jnp.float32).reshape(b, s, n_heads, -1).transpose(0, 2, 1, 3)

def _chunk(x):
    b, h, s = x.shape[:3]
    return x.reshape(b, h, s // CHUNK, CHUNK, *x.shape[3:])

def _flip(x):
    return jnp.flip(x, axis=2)

def _conv_centred(x, w):
    c = x.shape[-1]
    rhs = w.astype(jnp.float32).T[:, None, :]
    return lax.conv_general_dilated(x, rhs, window_strides=(1,),
                                    padding=[(CONV_K // 2, CONV_K // 2)],
                                    dimension_numbers=("NWC", "WIO", "NWC"),
                                    feature_group_count=c)

def _gated_delta_rule(q, k, v, g, beta):
    b_, h_, s_, dk = q.shape
    dv = v.shape[-1]
    q, k, v, g, beta = (_chunk(a) for a in (q, k, v, g, beta))
    g = jnp.cumsum(g, axis=-1)
    incl = jnp.tril(jnp.ones((CHUNK, CHUNK), dtype=bool))
    strict = jnp.tril(jnp.ones((CHUNK, CHUNK), dtype=bool), k=-1)
    decay = jnp.exp(jnp.where(incl, g[..., :, None] - g[..., None, :], -jnp.inf))
    k_beta = k * beta[..., None]
    a_mat = jnp.where(strict, jnp.einsum("bhncd,bhnsd->bhncs", k_beta, k) * decay, 0.0)
    eye = jnp.eye(CHUNK, dtype=q.dtype)
    t_mat = lax.linalg.triangular_solve(eye + a_mat, jnp.broadcast_to(eye, a_mat.shape),
                                        left_side=True, lower=True)
    u = jnp.einsum("bhncs,bhnse->bhnce", t_mat, v * beta[..., None])
    w = jnp.einsum("bhncs,bhnsd->bhncd", t_mat, k_beta * jnp.exp(g)[..., None])
    qk = jnp.where(incl, jnp.einsum("bhncd,bhnsd->bhncs", q, k) * decay, 0.0)
    q_dec = q * jnp.exp(g)[..., None]
    k_dec = k * jnp.exp(g[..., -1:] - g)[..., None]
    g_tot = jnp.exp(g[..., -1])

    def step(state, inp):
        u_c, w_c, qk_c, qd_c, kd_c, gt_c = inp
        v_new = u_c - jnp.einsum("bhcd,bhde->bhce", w_c, state)
        o_c = (jnp.einsum("bhcd,bhde->bhce", qd_c, state)
               + jnp.einsum("bhcs,bhse->bhce", qk_c, v_new))
        state = state * gt_c[..., None, None] + jnp.einsum("bhcd,bhce->bhde", kd_c, v_new)
        return state, o_c

    xs = tuple(jnp.moveaxis(a, 2, 0) for a in (u, w, qk, q_dec, k_dec, g_tot))
    _, o = lax.scan(step, jnp.zeros((b_, h_, dk, dv), q.dtype), xs)
    return jnp.moveaxis(o, 0, 2).reshape(b_, h_, s_, dv)

def _mlstm(q, k, v, i_pre, f_pre):
    b_, h_, s_, dk = q.shape
    dv = v.shape[-1]
    q, k, v, i_pre, f_pre = (_chunk(a) for a in (q, k, v, i_pre, f_pre))
    incl = jnp.tril(jnp.ones((CHUNK, CHUNK), dtype=bool))
    bcum = jnp.cumsum(jax.nn.log_sigmoid(f_pre), axis=-1)
    d_log = jnp.where(incl, bcum[..., :, None] - bcum[..., None, :] + i_pre[..., None, :], -jnp.inf)
    m_intra = jnp.max(d_log, axis=-1)
    p = jnp.exp(d_log - m_intra[..., None]) * jnp.einsum("bhncd,bhnsd->bhncs", q, k)
    num_intra = jnp.einsum("bhncs,bhnse->bhnce", p, v)
    den_intra = jnp.sum(p, axis=-1)
    b_last = bcum[..., -1]
    w_log = b_last[..., None] - bcum + i_pre
    m_w = jnp.max(w_log, axis=-1)
    wgt = jnp.exp(w_log - m_w[..., None])
    dc = jnp.einsum("bhnc,bhncd,bhnce->bhnde", wgt, k, v)
    dn = jnp.einsum("bhnc,bhncd->bhnd", wgt, k)

    def step(carry, inp):
        c_st, n_st, m_st = carry
        q_c, b_c, mi_c, num_c, den_c, bl_c, mw_c, dc_c, dn_c = inp
        inter_log = b_c + m_st[..., None]
        m_t = jnp.maximum(inter_log, mi_c)
        s_inter = jnp.exp(inter_log - m_t)
        s_intra = jnp.exp(mi_c - m_t)
        num = (s_inter[..., None] * jnp.einsum("bhcd,bhde->bhce", q_c, c_st)
               + s_intra[..., None] * num_c)
        den = s_inter * jnp.einsum("bhcd,bhd->bhc", q_c, n_st) + s_intra * den_c
        h = num / jnp.maximum(jnp.abs(den), jnp.exp(-m_t))[..., None]
        m_new = jnp.maximum(bl_c + m_st, mw_c)
        s_old = jnp.exp(bl_c + m_st - m_new)
        s_new = jnp.exp(mw_c - m_new)
        c_st = s_old[..., None, None] * c_st + s_new[..., None, None] * dc_c
        n_st = s_old[..., None] * n_st + s_new[..., None] * dn_c
        return (c_st, n_st, m_new), h

    xs = tuple(jnp.moveaxis(a, 2, 0) for a in
               (q, bcum, m_intra, num_intra, den_intra, b_last, m_w, dc, dn))
    init = (jnp.zeros((b_, h_, dk, dv), q.dtype), jnp.zeros((b_, h_, dk), q.dtype),
            jnp.zeros((b_, h_), q.dtype))
    _, h = lax.scan(step, init, xs)
    return jnp.moveaxis(h, 0, 2).reshape(b_, h_, s_, dv)

def _gdn_group(q, k, v, z, a, bb, conv_w, a_log, dt_bias, norm_g):
    bsz, s, _ = q.shape
    qkv = jax.nn.silu(_conv_centred(jnp.concatenate([q, k, v], axis=-1).astype(jnp.float32), conv_w))
    qh = _l2norm(_to_heads(qkv[..., :GDN_QK], GDN_HEADS)) * (GDN_DK ** -0.5)
    kh = _l2norm(_to_heads(qkv[..., GDN_QK:2 * GDN_QK], GDN_HEADS))
    vh = _to_heads(qkv[..., 2 * GDN_QK:], GDN_HEADS)
    a = a.astype(jnp.float32).reshape(bsz, s, N_DIR, GDN_HEADS)
    bb = bb.astype(jnp.float32).reshape(bsz, s, N_DIR, GDN_HEADS)
    g = -jnp.exp(a_log.astype(jnp.float32)) * jax.nn.softplus(a + dt_bias.astype(jnp.float32))
    beta = jax.nn.sigmoid(bb)
    g = g.transpose(2, 0, 3, 1)
    beta = beta.transpose(2, 0, 3, 1)
    o_f = _gated_delta_rule(qh, kh, vh, g[0], beta[0])
    o_b = _flip(_gated_delta_rule(_flip(qh), _flip(kh), _flip(vh), _flip(g[1]), _flip(beta[1])))
    o = (o_f + o_b).transpose(0, 2, 1, 3)
    o = o * lax.rsqrt(jnp.mean(o * o, axis=-1, keepdims=True) + EPS) * norm_g.astype(jnp.float32)
    return o.reshape(bsz, s, GDN_V) * jax.nn.silu(z.astype(jnp.float32))

def _mlstm_group(q, k, v, o_gate, i_in, f_in, i_bias, f_bias, norm_g):
    bsz, s, _ = q.shape
    qh = _to_heads(q, MLSTM_HEADS)
    kh = _to_heads(k, MLSTM_HEADS) * (MLSTM_DK ** -0.5)
    vh = _to_heads(v, MLSTM_HEADS)
    i_pre = (i_in.astype(jnp.float32).reshape(bsz, s, N_DIR, MLSTM_HEADS)
             + i_bias.astype(jnp.float32)).transpose(2, 0, 3, 1)
    f_pre = (f_in.astype(jnp.float32).reshape(bsz, s, N_DIR, MLSTM_HEADS)
             + f_bias.astype(jnp.float32)).transpose(2, 0, 3, 1)
    h_f = _mlstm(qh, kh, vh, i_pre[0], f_pre[0])
    h_b = _flip(_mlstm(_flip(qh), _flip(kh), _flip(vh), _flip(i_pre[1]), _flip(f_pre[1])))
    h = (h_f + h_b).transpose(0, 2, 1, 3)
    h = (h * lax.rsqrt(jnp.mean(h * h, axis=-1, keepdims=True) + EPS)).reshape(bsz, s, ML_V)
    return h * norm_g.astype(jnp.float32) * jax.nn.sigmoid(o_gate.astype(jnp.float32))

def _peer(h, w_q, sub_keys, u_tab, v_tab):
    bsz, s, d = h.shape
    t = h.reshape(-1, d)
    n_tok = t.shape[0]
    qry = (t @ w_q).astype(jnp.float32).reshape(n_tok, PEER_HEADS, 2, PEER_DKEY // 2)
    scores = jnp.einsum("thpd,hpkd->thpk", qry, sub_keys.astype(jnp.float32))
    s_top, i_top = lax.top_k(scores, PEER_TOPK)
    cand = (s_top[:, :, 0, :, None] + s_top[:, :, 1, None, :]).reshape(n_tok, PEER_HEADS, -1)
    cand_idx = (i_top[:, :, 0, :, None] * PEER_NKEYS + i_top[:, :, 1, None, :]).reshape(n_tok, PEER_HEADS, -1)
    best, pos = lax.top_k(cand, PEER_TOPK)
    idx = jnp.take_along_axis(cand_idx, pos, axis=-1)
    gate = jax.nn.softmax(best, axis=-1)
    nb = n_tok // PEER_BLOCK

    def block_fn(args):
        tb, ib, gb = args
        u = u_tab[ib]
        act = jax.nn.gelu(jnp.einsum("td,thkd->thk", tb, u).astype(jnp.float32), approximate=False)
        vv = v_tab[ib]
        return jnp.einsum("thk,thkd->td", (gb * act).astype(vv.dtype), vv)

    out = lax.map(block_fn, (t.reshape(nb, PEER_BLOCK, d),
                             idx.reshape(nb, PEER_BLOCK, PEER_HEADS, PEER_TOPK),
                             gate.reshape(nb, PEER_BLOCK, PEER_HEADS, PEER_TOPK)))
    return out.reshape(bsz, s, d).astype(h.dtype)

def second_inputs(seed: int = 0) -> dict:
    key = jax.random.key(seed)
    ks = jax.random.split(key, 20)
    f32 = jnp.float32
    nrm = lambda k, shp, sc: jax.random.normal(k, shp, f32) * sc
    dt = jnp.exp(jax.random.uniform(ks[5], (DEPTH_2, N_DIR, GDN_HEADS), f32,
                                    np.log(1e-3).astype(np.float32), np.log(1e-1).astype(np.float32)))
    return {
        "x": nrm(ks[0], (BATCH, SEQ, D_MODEL), 1.0),
        "norm1_g": 1.0 + nrm(ks[1], (DEPTH_2, D_MODEL), 0.02),
        "w_in": nrm(ks[2], (DEPTH_2, D_MODEL, D_IN), D_MODEL ** -0.5),
        "conv_w": nrm(ks[3], (DEPTH_2, 2 * GDN_QK + GDN_V, CONV_K), CONV_K ** -0.5),
        "gdn_a_log": jnp.log(jax.random.uniform(ks[4], (DEPTH_2, N_DIR, GDN_HEADS), f32, 1.0, 16.0)),
        "gdn_dt_bias": jnp.log(jnp.expm1(dt)),
        "gdn_norm_g": 1.0 + nrm(ks[6], (DEPTH_2, GDN_DV), 0.02),
        "mlstm_i_bias": nrm(ks[7], (DEPTH_2, N_DIR, MLSTM_HEADS), 0.1),
        "mlstm_f_bias": jax.random.uniform(ks[8], (DEPTH_2, N_DIR, MLSTM_HEADS), f32, 3.0, 6.0),
        "mlstm_norm_g": 1.0 + nrm(ks[9], (DEPTH_2, ML_V), 0.02),
        "w_out": nrm(ks[10], (DEPTH_2, D_MIX, D_MODEL), D_MIX ** -0.5),
        "norm2_g": 1.0 + nrm(ks[11], (DEPTH_2, D_MODEL), 0.02),
        "peer_wq": nrm(ks[12], (DEPTH_2, D_MODEL, PEER_HEADS * PEER_DKEY), D_MODEL ** -0.5),
        "peer_keys": nrm(ks[13], (DEPTH_2, PEER_HEADS, 2, PEER_NKEYS, PEER_DKEY // 2), (PEER_DKEY // 2) ** -0.5),
        "peer_u": nrm(ks[14], (DEPTH_2, PEER_N, D_MODEL), D_MODEL ** -0.5),
        "peer_v": nrm(ks[15], (DEPTH_2, PEER_N, D_MODEL), PEER_HEADS ** -0.5),
        "normf_g": 1.0 + nrm(ks[16], (D_MODEL,), 0.02),
    }

def second_block(x, norm1_g, w_in, conv_w, gdn_a_log, gdn_dt_bias, gdn_norm_g, mlstm_i_bias,
              mlstm_f_bias, mlstm_norm_g, w_out, norm2_g, peer_wq, peer_keys, peer_u, peer_v,
              normf_g):
    offsets = [int(o) for o in np.cumsum(SPLIT_SIZES)[:-1]]
    for l in range(DEPTH_2):
        h = _rmsnorm(x, norm1_g[l])
        p = h @ w_in[l]
        (gq, gk, gv, gz, ga, gb, mq, mk, mv, mo, mi, mf) = jnp.split(p, offsets, axis=-1)
        y_a = _gdn_group(gq, gk, gv, gz, ga, gb, conv_w[l], gdn_a_log[l], gdn_dt_bias[l], gdn_norm_g[l])
        y_b = _mlstm_group(mq, mk, mv, mo, mi, mf, mlstm_i_bias[l], mlstm_f_bias[l], mlstm_norm_g[l])
        y = jnp.concatenate([y_a, y_b], axis=-1).astype(x.dtype)
        x = x + y @ w_out[l]
        h2 = _rmsnorm(x, norm2_g[l])
        x = x + _peer(h2, peer_wq[l], peer_keys[l], peer_u[l], peer_v[l])
    return _rmsnorm(x, normf_g)


def setup_inputs(seed=0):
    out = dict(first_inputs(seed))
    for name, value in second_inputs(seed + 1).items():
        if name != "x":
            out[name + "_2"] = value
    return out


def reference(
    x, ln_ffn1, w_ffn1_gu, w_ffn1_down, ln_mix, w_in, pool_w, pool_scale, w_pool_branch, q_norm,
    k_norm, sinks, w_attn_branch, w_out, ln_ffn2, w_ffn2_gu, w_ffn2_down, norm1_g_2, w_in_2,
    conv_w_2, gdn_a_log_2, gdn_dt_bias_2, gdn_norm_g_2, mlstm_i_bias_2, mlstm_f_bias_2,
    mlstm_norm_g_2, w_out_2, norm2_g_2, peer_wq_2, peer_keys_2, peer_u_2, peer_v_2, normf_g_2,
):
    x = first_block(
        x, ln_ffn1, w_ffn1_gu, w_ffn1_down, ln_mix, w_in, pool_w, pool_scale, w_pool_branch,
        q_norm, k_norm, sinks, w_attn_branch, w_out, ln_ffn2, w_ffn2_gu, w_ffn2_down,
    )
    return second_block(
        x, norm1_g_2, w_in_2, conv_w_2, gdn_a_log_2, gdn_dt_bias_2, gdn_norm_g_2,
        mlstm_i_bias_2, mlstm_f_bias_2, mlstm_norm_g_2, w_out_2, norm2_g_2, peer_wq_2,
        peer_keys_2, peer_u_2, peer_v_2, normf_g_2,
    )


_drawn_inputs = setup_inputs


def setup_inputs(seed=0):
    import zlib

    import numpy as np

    out = dict(_drawn_inputs(seed))
    spreads = {}
    factors = {'q_norm': 4.298,
     'k_norm': 4.108,
     'sinks': 5.077,
     'gdn_norm_g_2': 14.608,
     'mlstm_i_bias_2': 24.235,
     'mlstm_norm_g_2': 18.339,
     'norm2_g_2': 9.002,
     'normf_g_2': 7.499}
    for name, (base, spread) in spreads.items():
        noise = np.random.default_rng([zlib.crc32(name.encode()), seed]).standard_normal(out[name].shape)
        drawn = base * np.exp(spread * noise) if base else spread * noise
        out[name] = __import__('jax').numpy.asarray(drawn.astype(out[name].dtype))
    for name, factor in factors.items():
        out[name] = (out[name] * factor).astype(out[name].dtype)
    return out
```

```python
from contextlib import ExitStack

import numpy as np

import concourse.bass as bass
from concourse import mybir

F32 = mybir.dt.float32
F32R = mybir.dt.float32r
U32 = mybir.dt.uint32
ALU = mybir.AluOpType
ACT = mybir.ActivationFunctionType
AX_X = mybir.AxisListType.X

P = 128
TOKENS = 512
TT = TOKENS // P
D = 1024
KB = D // P
FF = 2816
FB = FF // P
TILE = 16
HEADS, HD, KV_HEADS = 8, 64, 2
GROUP = HEADS // KV_HEADS
POOL_WINDOWS = (2, 4, 8, 16)
PAD = max(POOL_WINDOWS)
ROT = 16
THETA = 500000.0
EPS = 1e-6
GH = 4
CONV = 5
PEER_HEADS, NKEYS, TOPK = 8, 128, 16
LAYERS = 2

GU_TILES = FB
DOWN_TILES = FB * KB // TILE
FFN_TILES = GU_TILES + DOWN_TILES
IN_TILES = 13
MIX_TILES = IN_TILES + 2 + 2 + 4
LAYER_TILES = 2 * FFN_TILES + MIX_TILES
IN2_AT = LAYERS * LAYER_TILES
IN2_TILES = 17
OUT2_AT = IN2_AT + IN2_TILES
WQ_AT = OUT2_AT + 4
TABLE_AT = WQ_AT + 8
EG = 4
GROUPS = NKEYS // EG
CHUNK = 64
CHUNKS = TOKENS // CHUNK
AHEAD = 18
AHEAD_TILES = 2 * AHEAD
CHOICE_TILES = 6
QUAD_BUFS = 4
QUADS = TOKENS // 4
TILES = TABLE_AT + 4 * GROUPS


class Count:

    def __init__(self, eng, sem):
        self.eng, self.sem, self.n, self.i, self.per = eng, sem, 0, None, 0

    def value(self):
        return self.n if self.i is None else self.n + self.per * self.i

    def up(self, ins):
        self.n += 1
        ins.then_inc(self.sem, 1)
        return ins

    def held(self):
        self.eng.wait_ge(self.sem, self.value())

    def step(self, ins):
        self.up(ins)
        self.held()

    def loop(self, i, per):
        self.start, self.i, self.per = self.n, i, per

    def end(self, trips):
        assert self.n - self.start == self.per, (self.n, self.start, self.per)
        self.n, self.i = self.start + self.per * trips, None


def delta_signals(r):
    return 4 if r in (1, 4, 6) else 7


N_CONST = 7


def build(nc, x_in, weights, gains, small, pool_w, consts, rope, second, level_masks,
          keys, out):
    stack = ExitStack()
    with stack:
        sizes = {F32: 4, F32R: 4, U32: 4}
        offset = [0]

        def place(name, shape, dtype, at=None):
            nbytes = int(np.prod(shape[1:])) * sizes[dtype]
            if at is None:
                at = offset[0]
                offset[0] = -(-(at + nbytes) // 32) * 32
            return nc.alloc_sbuf_tensor_at(name, shape, dtype, offset=at + base)

        base = nc.sbuf_base if isinstance(nc.sbuf_base, int) else 0
        base = -(-base // 32) * 32
        sems = {}

        def sem(name):
            if name not in sems:
                sems[name] = stack.enter_context(nc.semaphore(name))
            return sems[name]

        x = place("x", [P, KB, TOKENS], F32)
        h_hi = place("h_hi", [P, KB, TOKENS], F32R)
        h_lo = place("h_lo", [P, KB, TOKENS], F32R)
        raw = place("raw", [P, 2, TILE * P], F32)
        w_hi = place("w_hi", [P, 2, TILE * P], F32R)
        w_lo = place("w_lo", [P, 2, TILE * P], F32R)
        rstd = place("rstd", [P, TOKENS], F32)
        sq = place("sq", [P, 2, TOKENS], F32)
        tmp = place("tmp", [P, TOKENS], F32)
        rcol = place("rcol", [P, 3, TT], F32)
        gain = place("gain", [P, 9, KB], F32)
        small_sb = place("small_sb", [P, LAYERS, 14], F32)
        const = place("const", [P, 5, P], F32)
        mask = place("mask", [P, 2 * P], F32)
        invc = place("invc", [P, 4, PAD], F32)
        headsel = place("headsel", [P, 2], F32)
        rope_sb = place("rope_sb", [P, 2, TOKENS], F32)
        region = offset[0]
        ident, swap, upper, lower, ones = (const[:, n, :] for n in range(5))

        offset[0] = region
        act_hi = place("act_hi", [P, FB, TOKENS], F32R)
        act_lo = place("act_lo", [P, FB, TOKENS], F32R)
        gate_s = place("gate_s", [P, TOKENS], F32)
        up_s = place("up_s", [P, TOKENS], F32)
        silu = place("silu", [P, TOKENS], F32)
        prod = up_s

        offset[0] = region
        pool_u = place("pool_u", [P, 4, PAD + TOKENS], F32)
        pool_s = place("pool_s", [P, 2, PAD + TOKENS], F32)
        qk = place("qk", [P, 5, TOKENS], F32)
        v_tok = place("v_tok", [P, TT, P], F32)
        probs_t0 = place("probs_t0", [P, 2, TOKENS], F32)
        gates = place("gates", [P, 2 * KB, TOKENS], F32)
        mix_late = place("mix_late", [P, 4, 2, TOKENS], F32R, at=offset[0] - KB * TOKENS * 4)
        att_hi = place("att_hi", [P, 4, TOKENS], F32R)
        att_lo = place("att_lo", [P, 4, TOKENS], F32R)
        y_hi = place("y_hi", [P, 4, TOKENS], F32R)
        y_lo = place("y_lo", [P, 4, TOKENS], F32R)
        pool_w_sb = place("pool_w_sb", [P, 4, P], F32)
        rq = place("rq", [P, 3, TT, 10], F32)
        soft = place("soft", [P, 2, 6, 4], F32)

        offset[0] = region
        gt = place("gt", [P, TT, 32], F32)
        g_abs = place("g_abs", [P, TT, 32], F32)
        g_log = place("g_log", [P, TT, 32], F32)
        gbias = place("gbias", [P, 40], F32)
        decay = place("decay", [P, TT, 8], F32)
        logf = place("logf", [P, TT, 8], F32)
        beta = place("beta", [P, TT, 8], F32)
        sums = place("sums", [P, 3, TT, 8], F32)
        e_in = place("e_in", [P, TT, 8], F32)
        e_out = place("e_out", [P, TT, 8], F32)
        e_all = place("e_all", [P, TT, 8], F32)
        a_col = place("a_col", [P, TT, 8], F32)
        floor = place("floor", [P, TT, 8], F32)
        den = place("den", [P, 2, TT], F32)
        conv_sb = place("conv_sb", [P, 12, CONV], F32)
        head_gain = place("head_gain", [P, 8], F32)
        r3 = place("r3", [P, 3, TT, 8], F32)
        rn = place("rn", [P, 3, 32], F32)
        m_row = place("m_row", [GH, 2, TOKENS], F32)
        masks2 = place("masks2", [P, 9, P], F32)
        h_ml = place("h_ml", [P, TT, GH, P], F32)
        o_gdn = place("o_gdn", [P, TT, GH, P], F32)
        gq = place("gq", [P, GH, TOKENS], F32)
        gk = place("gk", [P, GH, TOKENS], F32)
        shared = offset[0]
        p_t = place("p_t", [P, 2, TT, TOKENS], F32)
        overlay = offset[0]
        offset[0] = shared
        v_rows = place("v_rows", [P, TT, GH, P], F32)
        k_rows = place("k_rows", [P, TT, GH, P], F32)
        assert offset[0] == overlay
        mq = place("mq", [P, GH, TOKENS], F32)
        mk = place("mk", [P, GH, TOKENS], F32)
        mv = place("mv", [P, TT, GH, P + 2], F32)
        conv_in = place("conv_in", [P, 2, TOKENS + CONV - 1], F32, at=region - 2 * (TOKENS + CONV - 1) * 4)
        gv = place("gv", [P, GH, TOKENS], F32)
        offset[0] = overlay
        item_bufs = [[place(f"{name}{n}", [P, GH, P], F32)
                      for name in ("a_t", "inv", "b_t", "prod_y", "inv_t", "q_mask", "q_in", "k_out")]
                     for n in range(2)]
        state = place("state", [P, 2, GH, P], F32, at=region - 2 * GH * P * 4)
        offset[0] = overlay
        y2_hi = place("y2_hi", [P, KB, TOKENS], F32R)
        y2_lo = place("y2_lo", [P, KB, TOKENS], F32R)
        a_row = tmp

        offset[0] = region
        chosen = place("chosen", [P, 3, TOKENS], F32)
        numbers = place("numbers", [P, P], F32)
        stage = place("stage", [P, 2, 2, TOKENS], F32)
        kept = offset[0]
        qry = place("qry", [P, 2 * PEER_HEADS, TOKENS], F32)
        keys_sb = place("keys_sb", [P, 2 * PEER_HEADS, P], F32)
        sc = place("sc", [P, 2, 2 * PEER_HEADS, P], F32)
        top = place("top", [P, 2 * PEER_HEADS, TOPK], F32)
        top_at = place("top_at", [P, 2 * PEER_HEADS, TOPK], U32)
        top_key = place("top_key", [P, 2 * PEER_HEADS, TOPK], F32)
        cand = place("cand", [P, PEER_HEADS, TOPK, TOPK], F32)
        cand_rest = place("cand_rest", [P, PEER_HEADS, TOPK, TOPK], F32)
        best = place("best", [P, PEER_HEADS, TOPK], F32)
        best_at = place("best_at", [P, PEER_HEADS, TOPK], U32)
        pair_at = place("pair_at", [P, 2, PEER_HEADS, TOPK], U32)
        pair_f = place("pair_f", [P, 2, PEER_HEADS, TOPK], F32)
        picks = cand_rest
        sel = place("sel", [P, 3, PEER_HEADS, TOPK], F32)
        gate_sum = place("gate_sum", [P, 2, PEER_HEADS], F32)

        offset[0] = kept
        hot = place("hot", [P, QUAD_BUFS, 4, 2, P], F32)
        g_buf = place("g_buf", [P, 2, NKEYS, CHUNK], F32)

        offset[0] = kept
        g_in = place("g_in", [P, 2, CHUNKS, EG, CHUNK], F32)
        s_in = place("s_in", [P, 2, EG, TOKENS], F32)
        w_mix_hi = place("w_mix_hi", [P, 2, EG, TOKENS], F32R)
        w_mix_lo = place("w_mix_lo", [P, 2, EG, TOKENS], F32R)
        s_scaled = place("s_scaled", [P, TOKENS], F32)
        gelu = place("gelu", [P, TOKENS], F32)
        weighed = place("weighed", [P, TOKENS], F32)
        g_store = nc.dram_tensor("g_store", [GROUPS, CHUNKS, NKEYS, EG * CHUNK], F32, kind="Internal").ap()

        s_store = nc.dram_tensor("s_store", [AHEAD_TILES, NKEYS, 2, TOKENS], F32, kind="Internal").ap()

        scores = [pool_u[:, 2 * n:2 * n + 2, 0:TOKENS].rearrange("p a (b k) -> p a b k", b=2)
                  for n in range(2)]
        mixed = [(y_hi[:, n, :], y_lo[:, n, :]) if n < 4 else (mix_late[:, n - 4, 0, :], mix_late[:, n - 4, 1, :])
                 for n in range(KB)]
        probs_t = [probs_t0[:, :, :], pool_s[:, :, 0:TOKENS]]

        quad_banks = (6, 7, 2, 3)
        banks = [stack.enter_context(nc.psum_tensor(f"bank{n}", [P, 512], F32)) for n in range(8)]

        tile_landed = [sem("tile_landed0"), sem("tile_landed1")]
        hi_written, lo_written, tile_used = sem("hi_written"), sem("lo_written"), sem("tile_used")

        def ffn_of(f):
            layer, second = divmod(f, 2)
            return (layer * LAYER_TILES + second * (FFN_TILES + MIX_TILES), 3 * layer + 2 * second)

        def mix_of(layer):
            return layer * LAYER_TILES + FFN_TILES, 3 * layer + 1

        update_end = [FFN_TILES, FFN_TILES + MIX_TILES, LAYER_TILES,
                      LAYER_TILES + FFN_TILES, LAYER_TILES + FFN_TILES + MIX_TILES,
                      2 * LAYER_TILES, OUT2_AT + 4]
        update_base = [sum(delta_signals(q) for q in range(r)) for r in range(8)]

        def wait_delta(eng, r, n):
            if delta_signals(r) == 7:
                if n < 7:
                    eng.wait_ge(sem("delta_done"), update_base[r] + n + 1)
                else:
                    eng.wait_ge(tile_used, update_end[r])
            elif n % 2 == 0:
                eng.wait_ge(sem("delta_done"), update_base[r] + n // 2 + 1)
            else:
                eng.wait_ge(tile_used, update_end[r] - 4 + n // 2 + 1)

        block = stack.enter_context(nc.Block())

        def item_of(m):
            return m % 2, (m // 2 if m % 2 == 0 else TT - 1 - m // 2)

        def u_tile(g):
            return TABLE_AT + (2 * g if g < AHEAD else 4 * g - 2)

        def v_tile(g):
            if g < AHEAD - 1:
                return TABLE_AT + AHEAD_TILES + 2 * g
            return TABLE_AT + 4 * g + (4 if g < GROUPS - 1 else 2)

        def inv_t_index(pair, level, m):
            return 14 * pair + 2 * level + m % 2

        def level_index(pair, level, m):
            return 12 * pair + 2 * (level - 1) + m % 2

        def unit_of(u):
            return u % 2, u // 2

        def span(direction, a):
            return (a * P, TOKENS) if direction == 0 else (0, (a + 1) * P)

        @block.sync
        def _(sp):
            sp.dma_start(raw[:, 0, :], weights[0]).then_inc(tile_landed[0], 16)
            sp.dma_start(x[:, :, :], x_in).then_inc(sem("x_landed"), 16)
            sp.dma_start(raw[:, 1, :], weights[1]).then_inc(tile_landed[1], 16)
            with sp.Fori(0, (TILES - 2) // 2) as i:
                for slot in range(2):
                    source = sp.snap(2 * i + (2 + slot))
                    sp.wait_ge(lo_written, 2 * i + (slot + 1))
                    sp.dma_start(raw[:, slot, :], weights[source]).then_inc(tile_landed[slot], 16)
            sp.wait_ge(lo_written, TILES - 2)
            sp.dma_start(raw[:, 0, :], weights[TILES - 1]).then_inc(tile_landed[0], 16)

            for n in range(KB):
                sp.wait_ge(sem("result_written"), n + 1)
                sp.dma_start(out[:, n, :], x[:, n, :]).then_inc(sem("out_written"), 16)
            sp.wait_ge(sem("out_written"), 16 * KB)

        @block.gpsimd
        def _(pool):
            with pool.Fori(0, TILES // 2) as i:
                for slot in range(2):
                    pool.wait_ge(hi_written, 2 * i + (slot + 1))
                    pool.tensor_tensor(w_lo[:, slot, :], raw[:, slot, :],
                                       w_hi[:, slot, :].bitcast(F32), ALU.subtract).then_inc(lo_written, 1)
            pool.wait_ge(hi_written, TILES)
            pool.tensor_tensor(w_lo[:, 0, :], raw[:, 0, :], w_hi[:, 0, :].bitcast(F32),
                               ALU.subtract).then_inc(lo_written, 1)

        @block.scalar
        def _(act):
            act_local = Count(act, sem("act_local"))
            c_h_hi = Count(act, sem("h_hi_written"))
            c_sq = Count(act, sem("squares_written"))
            c_std = Count(act, sem("deviation_written"))
            c_silu = Count(act, sem("silu_written"))
            c_act_hi = Count(act, sem("act_hi_written"))
            c_qsq = Count(act, sem("head_squares_written"))
            c_qstd = Count(act, sem("head_deviation_written"))
            c_yhi = Count(act, sem("y_hi_written"))
            c_exp = Count(act, sem("exp_written"))
            c_pt = Count(act, sem("probs_t_written"))
            c_att = Count(act, sem("att_hi_written"))
            c_sig = Count(act, sem("sigmoid_written"))
            c_mix = Count(act, sem("mix_hi_written"))

            def split_hi(tile, i=None, per=2):
                if i is None and tile >= TILES:
                    return
                slot, half = tile % 2, tile // 2
                act.wait_ge(tile_landed[slot], 16 * (half + 1) if i is None else i * (8 * per) + 16 * (half + 1))
                if tile >= 2:
                    act.wait_ge(tile_used, tile - 1 if i is None else i * per + (tile - 1))
                act.activation(w_hi[:, slot, :], raw[:, slot, :], ACT.Copy).then_inc(hi_written, 1)

            def norm_operand(k, next_tile):
                for n in range(KB):
                    if k == 0:
                        act.wait_ge(sem("x_landed"), 16)
                        act.wait_ge(sem("const_landed"), 16 * N_CONST)
                    else:
                        act.wait_ge(sem("x_updated"), KB * (k - 1) + n + 1)
                    c_h_hi.up(act.activation(h_hi[:, n, :], x[:, n, :], ACT.Copy, scale=gain[:, k, n:n + 1]))
                    if KB * k + n >= 2:
                        act.wait_ge(sem("squares_summed"), KB * k + n - 1)
                    c_sq.up(act.activation(sq[:, n % 2, :], x[:, n, :], ACT.Square))
                    if n == 3:
                        split_hi(next_tile)
                act.wait_ge(sem("variance_written"), k + 1)
                c_std.up(act.activation(rcol[:, 1, :], rcol[:, 0, :], ACT.Sqrt))

            def ffn(f):
                t0, k = ffn_of(f)
                norm_operand(k, t0 + 1)

                def activate(s, i=None):
                    at = s if i is None else i * 2 + s
                    act.wait_ge(sem("gate_scaled"), at + (FB * f + 1))
                    c_silu.up(act.activation(silu[:, :], gate_s[:, :], ACT.Silu))
                    act.wait_ge(sem("prod_written"), at + (FB * f + 1))
                    if i is not None:
                        act.wait_ge(sem("x_landed"), 16)
                    c_act_hi.up(act.activation(act_hi[:, at, :], prod[:, :], ACT.Copy))

                activate(0)
                split_hi(t0 + 2)
                activate(1)
                loops = (c_silu, c_act_hi)
                with act.Fori(0, (FB - 2) // 2) as i:
                    for c in loops:
                        c.loop(i, 2)
                    for u in range(2):
                        split_hi(t0 + 3 + u, i)
                        activate(2 + u, i)
                for c in loops:
                    c.end((FB - 2) // 2)
                with act.Fori(0, 5) as i:
                    for u in range(2):
                        split_hi(t0 + 23 + u, i)
                split_hi(t0 + 33)

            def mix(layer):
                tm, k = mix_of(layer)
                act.wait_ge(tile_used, tm)
                act.dma_start(pool_w_sb[:, :, :], pool_w[layer]).then_inc(sem("pool_w_landed"), 16)
                norm_operand(k, tm + 1)

                def square_head(ci):
                    act.wait_ge(sem("column_read"), 26 * layer + 4 + ci + 1)
                    if ci >= 2:
                        act.wait_ge(sem("head_squares_summed"), 5 * layer + ci - 1)
                    else:
                        act.wait_ge(sem("squares_summed"), KB * (k + 1))
                    c_qsq.up(act.activation(sq[:, ci % 2, :], qk[:, ci, :], ACT.Square))

                def exps(u):
                    act.wait_ge(sem("max_written"), 8 * layer + u + 1)
                    b, lo = u % 2, 0 if u >= 2 else P
                    for g in range(GROUP):
                        act.activation(scores[b][:, g // 2, g % 2, lo:], scores[b][:, g // 2, g % 2, lo:],
                                       ACT.Exp, bias=soft[:, b, 1, g:g + 1],
                                       accum_out=soft[:, b, 3, g:g + 1])
                    c_exp.up(act.activation(soft[:, b, 5, :], soft[:, b, 2, :], ACT.Exp))

                def copy_probs(u):
                    act.wait_ge(sem("probs_turned"), 8 * layer + u + 1)
                    if u >= 2:
                        act.wait_ge(sem("values_done"), 8 * layer + u - 1)
                    for j in range(0 if u >= 2 else 1, 2):
                        ins = act.activation(probs_t[u % 2][:, j, :], banks[(1, 7)[j]][:, :], ACT.Copy)
                    c_pt.up(ins)

                def att_split(u):
                    act.wait_ge(sem("values_done"), 8 * layer + u + 1)
                    rows = slice(64 * (u % 2), 64 * (u % 2) + 64)
                    out_bank = banks[3 + 2 * (u % 2)][rows, :].rearrange("p (g q) -> p g q", g=4)
                    c_att.up(act.activation(att_hi[rows, :, u // 2 * P:u // 2 * P + P], out_bank, ACT.Copy))

                for s in range(IN_TILES):
                    if s > 0:
                        split_hi(tm + s + 1)
                    if s == 2:
                        square_head(0)
                        square_head(1)
                    if s == 3:
                        square_head(2)
                        square_head(3)
                    if s == 4:
                        square_head(4)
                    if s == 5:
                        act.wait_ge(sem("head_variance_written"), layer + 1)
                        c_qstd.up(act.activation(rq[:, 1], rq[:, 0], ACT.Sqrt))
                        for g in range(4):
                            act.wait_ge(sem("pool_product_done"), 4 * layer + g + 1)
                            c_yhi.up(act.activation(y_hi[:, g, :], banks[3 + g][:, :], ACT.Copy,
                                                    scale=small_sb[:, layer, 2 + g:3 + g]))
                    if s >= 10:
                        att_split(2 * (s - 10))
                        att_split(2 * (s - 10) + 1)
                    if 9 <= s:
                        copy_probs(2 * (s - 9))
                        copy_probs(2 * (s - 9) + 1)
                    if 8 <= s <= 11:
                        exps(2 * (s - 8))
                        exps(2 * (s - 8) + 1)
                att_split(6)
                att_split(7)
                split_hi(tm + 14)
                for n in range(2 * KB):
                    act.wait_ge(sem("column_read"), 26 * layer + 10 + n + 1)
                    c_sig.up(act.activation(gates[:, n, :], gates[:, n, :], ACT.Sigmoid))
                split_hi(tm + 15)
                split_hi(tm + 16)
                split_hi(tm + 17)
                for n in range(KB):
                    act.wait_ge(sem("mixed"), KB * layer + n + 1)
                    c_mix.up(act.activation(mixed[n][0], gates[:, n, :], ACT.Copy))
                for n in range(18, 22):
                    split_hi(tm + n)


            def second_mixer():
                k = 6
                act.wait_ge(tile_used, IN2_AT)
                act.dma_start(gbias[:, :], second[:, 0:40]).then_inc(sem("second_landed"), 16)
                act.dma_start(conv_sb[:, :, :], second[:, 40:100].rearrange("p (a b) -> p a b", b=CONV)).then_inc(
                    sem("second_landed"), 16)
                act.dma_start(head_gain[:, :], second[:, 100:108]).then_inc(sem("second_landed"), 16)
                act.dma_start(masks2[:, :, :], level_masks[:, 0:9]).then_inc(sem("second_landed"), 16)
                norm_operand(k, IN2_AT + 1)
                c_g = Count(act, sem("gate_logs"))
                c_silu2 = Count(act, sem("conv_activated"))
                c_sq2 = Count(act, sem("qk_squares_written"))
                c_pexp = Count(act, sem("p_exp_written"))

                act.wait_ge(sem("gates_read"), 1)
                c_g.step(act.activation(g_log[:, :, :], g_abs[:, :, :], ACT.Exp))
                c_g.step(act.activation(g_log[:, :, :], g_log[:, :, :], ACT.Ln, bias=1.0))
                c_g.step(act.activation(gbias[:, 32:40], gbias[:, 32:40], ACT.Exp))
                c_g.step(act.activation(beta[:, :, :], gt[:, :, 8:16], ACT.Sigmoid))

                def conv_silu(c):
                    act.wait_ge(sem("convolved"), c + 1)
                    dst = (gq, gk, gv)[c // 4][:, c % 4, :]
                    c_silu2.step(act.activation(dst, dst, ACT.Silu))

                def square(c):
                    if c == 0:
                        act.wait_ge(sem("values2_turned"), 4)
                    if c >= 2:
                        act.wait_ge(sem("qk_squares_summed"), c - 1)
                    c_sq2.up(act.activation(sq[:, c % 2, :], (gq, gk)[c // 4][:, c % 4, :], ACT.Square))

                def unit_exp(u, tiles=range(TT)):
                    direction, h = unit_of(u)
                    for a in tiles:
                        lo, up = span(direction, a)
                        act.wait_ge(sem("p_args"), TT * u + a + 1)
                        c_pexp.up(act.activation(p_t[:, u % 2, a, lo:up], p_t[:, u % 2, a, lo:up], ACT.Exp,
                                                 scale=-1.0))

                for s in range(1, 13):
                    if s < 8:
                        split_hi(IN2_AT + s + 1)
                    if s == 2:
                        act.wait_ge(sem("sums_written"), 1)
                        c_g.up(act.activation(e_in[:, :, :], sums[:, 0], ACT.Exp))
                        c_g.up(act.activation(e_all[:, :, :], sums[:, 1], ACT.Exp))
                        c_g.up(act.activation(e_out[:, :, :], e_out[:, :, :], ACT.Exp))
                    if s == 5:
                        act.wait_ge(sem("floor_args"), 1)
                        c_g.step(act.activation(floor[:, :, :], floor[:, :, :], ACT.Exp, scale=-1.0))
                    if s >= 7:
                        unit_exp(s - 7, (0, 1))
                        if s >= 8:
                            split_hi(IN2_AT + s + 1)
                        unit_exp(s - 7, (2, 3))
                        for c in (2 * (s - 7), 2 * (s - 7) + 1):
                            conv_silu(c)
                            if c < 8:
                                square(c)
                unit_exp(6)
                unit_exp(7)
                act.wait_ge(sem("qk_variance"), 1)
                act.activation(r3[:, 1], r3[:, 0], ACT.Sqrt).then_inc(sem("qk_deviation"), 1)

                def square_heads(which, tiles, ready):
                    act.wait_ge(sem(("o_written", "h_written")[which]), ready)
                    for t in tiles:
                        for h in range(GH):
                            at = 16 * which + 4 * t + h
                            ins = act.activation(tmp[:, h * P:h * P + P], (o_gdn, h_ml)[which][:, t, h, :], ACT.Square,
                                                 accum_out=rn[:, 0, at:at + 1])
                            act_local.up(ins)
                        act_local.held()

                square_heads(1, range(TT), 8)

                c_e = Count(act, sem("decay_exp"))
                c_y = Count(act, sem("level_copied"))
                c_vn = Count(act, sem("v_new_written"))

                for pair in range(4):
                    for m in (2 * pair, 2 * pair + 1):
                        a_t, inv, b_t, prod_y, inv_t, q_mask, q_in, k_out = item_bufs[m % 2]
                        act.wait_ge(sem("decay_args"), m + 1)
                        c_e.up(act.activation(prod_y[:, :, :], prod_y[:, :, :], ACT.Exp))
                        c_e.up(act.activation(b_t[:, :, :], banks[4 * (m % 2)][:, :].rearrange("p (h t) -> p h t", h=GH),
                                              ACT.Exp))
                    if pair == 3:
                        square_heads(0, (1, 2), 6)
                    for level in range(1, 7):
                        for m in (2 * pair, 2 * pair + 1):
                            prod_y = item_bufs[m % 2][3]
                            act.wait_ge(sem("level_y"), level_index(pair, level, m) + 1)
                            if level == 1:
                                act.wait_ge(sem("inv_t_written"), inv_t_index(pair, 0, m) + 1)
                            c_y.up(act.activation(prod_y[:, :, :],
                                                  banks[4 * (m % 2)][:, :].rearrange("p (h t) -> p h t", h=GH), ACT.Copy))
                    for m in (2 * pair, 2 * pair + 1):
                        act.wait_ge(sem("v_new_done"), m + 1)
                        c_vn.up(act.activation(item_bufs[m % 2][2][:, :, :],
                                               banks[4 * (m % 2) + 1][:, :].rearrange("p (h t) -> p h t", h=GH), ACT.Copy))

                square_heads(0, (0, TT - 1), 8)
                act.wait_ge(sem("out_variance"), 1)
                act.activation(rn[:, 1, :], rn[:, 0, :], ACT.Sqrt).then_inc(sem("out_deviation"), 1)
                c_z = Count(act, sem("z_activated"))
                c_y2 = Count(act, sem("y2_hi_written"))
                for j in range(8):
                    if j % 2 == 0:
                        split_hi(IN2_AT + 14 + j // 2)
                    act.wait_ge(sem("z_read"), j + 1)
                    zb = (gq, gk)[j % 2][:, 0, :]
                    c_z.up(act.activation(zb, zb, ACT.Silu if j < 4 else ACT.Sigmoid))
                    act.wait_ge(sem("y2_written"), j + 1)
                    c_y2.up(act.activation(y2_hi[:, j, :], (gq, gk)[j % 2][:, 1, :], ACT.Copy))
                for t in range(OUT2_AT + 1, OUT2_AT + 5):
                    split_hi(t)


            def experts():
                k = 7
                act.wait_ge(tile_used, WQ_AT)
                act.dma_start(keys_sb[:, :, :], keys).then_inc(sem("keys_landed"), 16)
                act.dma_start(numbers[:, :], level_masks[:, 9]).then_inc(sem("keys_landed"), 16)
                norm_operand(k, WQ_AT + 1)
                c_q = Count(act, sem("query_written"))
                c_sc = Count(act, sem("key_scores_written"))
                c_ge = Count(act, sem("gates_exp"))
                c_ev = Count(act, sem("quad_stored"))
                c_gelu = Count(act, sem("gelu_written"))
                c_st = Count(act, sem("s_staged"))
                c_wh = Count(act, sem("weighed_hi_written"))
                for s in range(8):
                    for half in range(2):
                        if half == 0:
                            act.wait_ge(sem("query_done"), s + 1)
                        else:
                            act.wait_ge(tile_used, WQ_AT + s + 1)
                        c_q.up(act.activation(qry[:, 2 * s + half, :], banks[(0, 2)[half]][:, :], ACT.Copy))
                    split_hi(WQ_AT + s + 2)

                def key_scores(t):
                    for quarter in range(4):
                        act.wait_ge(sem("key_scores_done"), 4 * t + quarter + 1)
                        if t >= 2:
                            act.wait_ge(sem("top_keys_written"), t - 1)
                        c_sc.up(act.activation(sc[:, t % 2, 4 * quarter:4 * quarter + 4, :],
                                               banks[3 + quarter % 2][:, :].rearrange("p (a b) -> p a b", a=4),
                                               ACT.Copy, scale=rcol[:, 2, t:t + 1]))

                s_stored = [sem("s_stored0"), sem("s_stored1")]

                def stage_row(n, e, i=None):
                    if e == 0:
                        act.wait_ge(sem("s_ahead_done"), n + 1 if i is None else i * 2 + (n + 1))
                        if n >= 2:
                            there = 16 * (n // 2)
                            act.wait_ge(s_stored[n % 2], there if i is None else i * 16 + there)
                    else:
                        act.wait_ge(tile_used, TABLE_AT + n + 1 if i is None else i * 2 + (TABLE_AT + n + 1))
                    c_st.up(act.activation(stage[:, n % 2, e, :], banks[e][:, :], ACT.Copy))

                def store_tile(n, i=None):
                    target = n if i is None else act.snap(i * 2 + n)
                    c_st.held()
                    act.dma_start(s_store[target], stage[:, n % 2]).then_inc(s_stored[n % 2], 16)
                    split_hi(TABLE_AT + n + 2, i)

                def ahead(n, i=None):
                    stage_row(n, 0, i)
                    stage_row(n, 1, i)
                    store_tile(n, i)

                key_scores(0)
                for t in range(TT):
                    n = CHOICE_TILES * t
                    if t + 1 < TT:
                        key_scores(t + 1)
                    ahead(n)
                    ahead(n + 1)
                    with act.Fori(0, (CHOICE_TILES - 4) // 2) as i:
                        c_st.loop(i, 4)
                        ahead(n + 2, i)
                        ahead(n + 3, i)
                    c_st.end((CHOICE_TILES - 4) // 2)
                    act.wait_ge(sem("gate_args_written"), t + 1)
                    c_ge.up(act.activation(sel[:, 2], sel[:, 2], ACT.Exp))
                    ahead(n + 4)
                    ahead(n + 5)

                stored = [sem("gates_stored0"), sem("gates_stored1")]
                for c in range(CHUNKS):
                    for half in range(2):
                        with act.Fori(0, CHUNK // 32) as i:
                            c_ev.loop(i, 4)
                            for b in range(4):
                                q = CHUNK // 4 * c + CHUNK // 8 * half + b
                                at = act.snap(i * 16 + (CHUNK // 2 * half + 4 * b))
                                act.wait_ge(sem("quad_done"), i * 4 + (q + 1))
                                if c >= 2:
                                    act.wait_ge(stored[c % 2], 16 * (c // 2))
                                else:
                                    act.wait_ge(sem("keys_landed"), 32)
                                c_ev.up(act.activation(
                                    g_buf[:, c % 2, :, bass.ds(at, 4)],
                                    banks[quad_banks[b]][:, :].rearrange("p (t i) -> p i t", t=4), ACT.Copy))
                        c_ev.end(CHUNK // 32)
                        stage_row(CHOICE_TILES * TT + c, half)
                    c_ev.held()
                    act.dma_start(g_store[:, c].rearrange("g j n -> j g n"),
                                  g_buf[:, c % 2].rearrange("p (g e) t -> p g (e t)", g=GROUPS)).then_inc(stored[c % 2], 16)
                    store_tile(CHOICE_TILES * TT + c)

                landed = [sem("gates_landed0"), sem("gates_landed1")]
                s_landed = [sem("s_landed0"), sem("s_landed1")]

                def load_group(g, i=None):
                    source = g if i is None else act.snap(i * 2 + g)
                    tile = 2 * g if i is None else act.snap(i * 4 + 2 * g)
                    if g >= 2 or i is not None:
                        act.wait_ge(sem("weighed_written"), EG * (g - 1) if i is None else i * (2 * EG) + EG * (g - 1))
                    act.dma_start(g_in[:, g % 2].rearrange("p c e t -> p c (e t)"),
                                  g_store[source].rearrange("c j n -> j c n")).then_inc(landed[g % 2], 16)
                    if g < AHEAD:
                        act.dma_start(s_in[:, g % 2].rearrange("p (a e) t -> p a (e t)", a=2),
                                      s_store[bass.ds(tile, 2)].rearrange("a j e t -> j a (e t)")).then_inc(
                                          s_landed[g % 2], 16)

                def chain(g, e, i=None):
                    at = EG * g + e + 1 if i is None else i * (2 * EG) + (EG * g + e + 1)
                    act.wait_ge(sem("s_scaled_written"), at)
                    c_gelu.up(act.activation(gelu[:, :], s_scaled[:, :], ACT.Gelu))
                    act.wait_ge(sem("weighed_written"), at)
                    c_wh.up(act.activation(w_mix_hi[:, g % 2, e, :], weighed[:, :], ACT.Copy))

                def early_step(g, i=None):
                    load_group(g + 1, i)
                    for e in range(EG):
                        chain(g, e, i)
                        if e >= 2 and g > 0:
                            split_hi(v_tile(g - 1) + e, i, 4)

                def step(g, i=None):
                    if g < GROUPS - 1:
                        load_group(g + 1, i)
                    after = u_tile(g) + 2
                    chain(g, 0, i)
                    split_hi(after, i, 8)
                    chain(g, 1, i)
                    chain(g, 2, i)
                    split_hi(after + 1, i, 8)
                    chain(g, 3, i)
                    split_hi(after + 2, i, 8)
                    split_hi(after + 3, i, 8)

                def looped(trips, g, body):
                    with act.Fori(0, trips) as i:
                        for c in (c_gelu, c_wh):
                            c.loop(i, 2 * EG)
                        body(g, i)
                        body(g + 1, i)
                    for c in (c_gelu, c_wh):
                        c.end(trips)

                last = CHOICE_TILES * TT + CHUNKS
                assert AHEAD_TILES == last + 4
                ahead(last)
                ahead(last + 1)
                for b in range(2):
                    act.wait_ge(stored[b], 16 * CHUNKS // 2)
                load_group(0)
                ahead(last + 2)
                early_step(0)
                ahead(last + 3)
                for b in range(2):
                    act.wait_ge(s_stored[b], 16 * AHEAD)
                looped((AHEAD - 2) // 2, 1, early_step)
                early_step(AHEAD - 1)
                looped((GROUPS - AHEAD - 2) // 2, AHEAD, step)
                step(GROUPS - 2)
                step(GROUPS - 1)

                k = 8
                for n in range(KB):
                    act.wait_ge(sem("x_updated"), KB * 7 + KB * (GROUPS - 1) + n + 1)
                    act.wait_ge(sem("squares_summed"), KB * k + n - 1)
                    c_sq.up(act.activation(sq[:, n % 2, :], x[:, n, :], ACT.Square))
                act.wait_ge(sem("variance_written"), k + 1)
                c_std.up(act.activation(rcol[:, 1, :], rcol[:, 0, :], ACT.Sqrt))

            act.dma_start(gain[:, :, :], gains).then_inc(sem("const_landed"), 16)
            act.dma_start(const[:, :, :], consts[:, 0:5 * P].rearrange("p (a b) -> p a b", a=5)).then_inc(
                sem("const_landed"), 16)
            act.dma_start(mask[:, :], consts[:, 5 * P:7 * P]).then_inc(sem("const_landed"), 16)
            act.dma_start(invc[:, :, :], consts[:, 7 * P:7 * P + 64].rearrange("p (a b) -> p a b", a=4)).then_inc(
                sem("const_landed"), 16)
            act.dma_start(headsel[:, :], consts[:, 7 * P + 64:7 * P + 66]).then_inc(sem("const_landed"), 16)
            act.dma_start(rope_sb[:, :, :], rope).then_inc(sem("const_landed"), 16)
            act.dma_start(small_sb[:, :, :], small).then_inc(sem("const_landed"), 16)
            split_hi(0)
            for layer in range(LAYERS):
                ffn(2 * layer)
                mix(layer)
                ffn(2 * layer + 1)
            second_mixer()
            experts()

        @block.tensor
        def _(pe):
            used = Count(pe, tile_used)
            c_delta = Count(pe, sem("delta_done"))
            c_gate = Count(pe, sem("gate_done"))
            c_stat = Count(pe, sem("squares_summed"))
            c_spread = Count(pe, sem("rstd_spread"))
            c_col = Count(pe, sem("column_done"))
            c_qsum = Count(pe, sem("head_squares_summed"))
            c_qspread = Count(pe, sem("head_rstd_spread"))
            c_swap = Count(pe, sem("swapped"))
            c_vt = Count(pe, sem("values_turned"))
            c_poolp = Count(pe, sem("pool_product_done"))
            c_scores = Count(pe, sem("scores_done"))
            c_turn = Count(pe, sem("probs_turned"))
            c_values = Count(pe, sem("values_done"))
            c_branch = Count(pe, sem("branch_done"))

            def product(out_ap, slot, blk, m_hi, m_lo, start, stop):
                cols = slice(blk * P, blk * P + P)
                pe.matmul(out_ap, w_hi[:, slot, cols], m_hi, start=start, stop=False)
                pe.matmul(out_ap, w_hi[:, slot, cols], m_lo, start=False, stop=False)
                return pe.matmul(out_ap, w_lo[:, slot, cols], m_hi, start=False, stop=stop)

            def column(bank, slot, c):
                for n in range(KB):
                    last = product(banks[bank][:, :], slot, 2 * n + c, h_hi[:, n, :], h_lo[:, n, :],
                                   n == 0, n == KB - 1)
                return last

            def wait_tile(tile, i=None, per=2):
                pe.wait_ge(lo_written, tile + 1 if i is None else i * per + (tile + 1))

            def first_column(k, tile, bank):
                wait_tile(tile)
                for n in range(KB):
                    pe.wait_ge(sem("h_lo_written"), KB * k + n + 1)
                    last = product(banks[bank][:, :], tile % 2, 2 * n, h_hi[:, n, :], h_lo[:, n, :],
                                   n == 0, n == KB - 1)
                    pe.wait_ge(sem("squares_written"), KB * k + n + 1)
                    if n == 0 and k > 0:
                        pe.wait_ge(sem("x_updated"), KB * (k - 1) + 2)
                    for t in range(TT):
                        ins = pe.matmul(banks[1][:, t:t + 1], sq[:, n % 2, t * P:t * P + P], ones[:, 0:1],
                                        start=(n == 0 and t == 0), stop=(n == KB - 1),
                                        skip_group_check=True)
                    c_stat.up(ins)
                return last

            def spread_rstd(k, bank):
                pe.wait_ge(sem("rcol_written"), k + 1)
                for t in range(TT):
                    ins = pe.matmul(banks[bank][:, t * P:t * P + P],
                                    rcol[:, 2, t:t + 1].to_broadcast([P, P]), ident, start=True, stop=True)
                c_spread.up(ins)

            def ffn(f):
                t0, k = ffn_of(f)
                if k > 0:
                    pe.wait_ge(sem("x_updated"), KB * (k - 1) + 1)
                last = first_column(k, t0, 0)
                c_gate.up(last)
                if k > 0:
                    pe.wait_ge(sem("x_updated"), KB * (k - 1) + 3)
                used.up(column(2, t0 % 2, 1))
                if k > 0:
                    pe.wait_ge(sem("x_updated"), KB * (k - 1) + 6)
                spread_rstd(k, 5)

                def step(s, i=None):
                    gate_bank, up_bank = ((0, 2), (3, 4))[s % 2]
                    at = s if i is None else i * 2 + s
                    wait_tile(t0 + s, i)
                    if s >= 2:
                        pe.wait_ge(sem("up_scaled"), at + (FB * f - 1))
                    c_gate.up(column(gate_bank, (t0 + s) % 2, 0))
                    used.up(column(up_bank, (t0 + s) % 2, 1))

                if k > 0:
                    pe.wait_ge(sem("x_updated"), KB * (k - 1) + 5)
                step(1)
                with pe.Fori(0, (FB - 2) // 2) as i:
                    for c in (c_gate, used):
                        c.loop(i, 2)
                    for u in range(2):
                        step(2 + u, i)
                for c in (c_gate, used):
                    c.end((FB - 2) // 2)

                def down(j, i=None, order=range(KB), first=False, final=False):
                    at = j if i is None else i * 2 + j
                    wait_tile(t0 + FB + j, i)
                    pe.wait_ge(sem("act_lo_written"), at * 2 + (FB * f + 2))
                    for n in order:
                        if first and n == 1:
                            pe.wait_ge(sem("variance_written"), k + 1)
                        if first and n == 5:
                            pe.wait_ge(sem("rstd_written"), k + 1)
                            if k > 0:
                                pe.wait_ge(sem("x_updated"), KB * k)
                        if first and n == 0:
                            pe.wait_ge(sem("up_scaled"), FB * f + FB - 1)
                        if first and n == 3:
                            pe.wait_ge(sem("up_scaled"), FB * f + FB)
                        for r in range(2):
                            last = product(banks[n][:, :], (t0 + FB + j) % 2, KB * r + n,
                                           act_hi[:, at * 2 + r, :], act_lo[:, at * 2 + r, :],
                                           first and r == 0, final and r == 1)
                        if final and n < KB - 1:
                            c_delta.up(last)
                    used.up(last)

                down(0, order=(1, 5, 6, 7, 0, 2, 3, 4), first=True)
                with pe.Fori(0, 4) as i:
                    used.loop(i, 2)
                    down(1, i)
                    down(2, i)
                used.end(4)
                down(9)
                down(10, final=True)

            def mix(layer):
                tm, k = mix_of(layer)
                xu = KB * (k - 1)

                def col(c):
                    tile = tm + c // 2
                    bank, slot = (0, 2)[c % 2], tile % 2
                    if c % 2 == 0:
                        wait_tile(tile)
                    pe.wait_ge(sem("column_read"), 26 * layer + c - 1)
                    last = column(bank, slot, c % 2)
                    (used if c % 2 else c_col).up(last)

                def sum_head_squares(ci):
                    pe.wait_ge(sem("head_squares_written"), 5 * layer + ci + 1)
                    for t in range(TT):
                        ins = pe.matmul(banks[3][:, 10 * t + 2 * ci:10 * t + 2 * ci + 2],
                                        sq[:, ci % 2, t * P:t * P + P], headsel[:, :], start=True, stop=True)
                    c_qsum.up(ins)

                def spread_head(ci):
                    bank = 4 + ci % 2
                    if ci == 0:
                        pe.wait_ge(sem("head_rcol_written"), layer + 1)
                        pe.wait_ge(sem("y_lo_written"), 4 * layer + 3)
                    if ci >= 2:
                        pe.wait_ge(sem("head_normed"), 5 * layer + ci - 1)
                    for t in range(TT):
                        for half in range(2):
                            ins = pe.matmul(banks[bank][HD * half:HD * half + HD, t * P:t * P + P],
                                            rq[:, 2, t, 2 * ci + half:2 * ci + half + 1].to_broadcast([P, HD]),
                                            ident, start=True, stop=True)
                    c_qspread.up(ins)

                def swap_head(ci):
                    bank = (6, 3)[ci % 2]
                    pe.wait_ge(sem("head_normed"), 5 * layer + ci + 1)
                    if ci == 0:
                        pe.wait_ge(sem("y_lo_written"), 4 * layer + 4)
                    if ci >= 2:
                        pe.wait_ge(sem("swap_scaled"), 5 * layer + ci - 1)
                    c_swap.up(pe.matmul(banks[bank][:, :], swap, qk[:, ci, :], start=True, stop=True))

                def score(u):
                    n, hk = divmod(u, 2)
                    rows = slice(64 * hk, 64 * hk + 64)
                    keys = slice((n - 1) * P if n else 0, n * P + P)
                    lo = 0 if n else P
                    if u == 0:
                        pe.wait_ge(sem("roped"), 5 * layer + 5)
                    if u >= 2:
                        pe.wait_ge(sem("scores_read"), 16 * layer + 2 * (u - 2) + 2)
                    if u >= 4:
                        pe.wait_ge(sem("att_lo_written"), 8 * layer + u - 3)
                    for g in range(GROUP):
                        at = (g % 2) * 2 * P + lo
                        ins = pe.matmul(banks[3 + 2 * hk + g // 2][:, at:(g % 2 + 1) * 2 * P],
                                        qk[rows, g, n * P:n * P + P], qk[rows, 4, keys], start=True, stop=True)
                    c_scores.up(ins)

                def turn(u):
                    pe.wait_ge(sem("probs_scaled"), 8 * layer + u + 1)
                    if u >= 1:
                        pe.wait_ge(sem("probs_t_written"), 8 * layer + u)
                    for j in range(0 if u >= 2 else 1, 2):
                        for g in range(GROUP):
                            ins = pe.transpose(banks[(1, 7)[j]][:, g * P:g * P + P],
                                               scores[u % 2][:, g // 2, g % 2, j * P:j * P + P], ident)
                    c_turn.up(ins)

                def values(u):
                    n, hk = divmod(u, 2)
                    rows = slice(64 * hk, 64 * hk + 64)
                    pe.wait_ge(sem("probs_t_written"), 8 * layer + u + 1)
                    pe.wait_ge(sem("scores_read"), 16 * layer + 2 * min(u + 2, 7) + 2)
                    if u >= 6:
                        pe.wait_ge(sem("att_lo_written"), 8 * layer + u - 1)
                    js = range(0 if n else 1, 2)
                    for j in js:
                        ins = pe.matmul(banks[3 + 2 * hk][rows, :], v_tok[:, n - 1 + j, rows],
                                        probs_t[u % 2][:, j, :], start=(j == js[0]), stop=(j == 1))
                    c_values.up(ins)

                pe.wait_ge(sem("x_updated"), xu + 1)
                c_col.up(first_column(k, tm, 0))
                pe.wait_ge(sem("x_updated"), xu + 3)
                used.up(column(2, tm % 2, 1))
                pe.wait_ge(sem("x_updated"), xu + 8)
                spread_rstd(k, 7)
                for s in range(1, IN_TILES):
                    col(2 * s)
                    if s == 5:
                        pe.wait_ge(sem("column_read"), 26 * layer + 10)
                        for t in range(TT):
                            ins = pe.transpose(banks[7][:, t * P:t * P + P], tmp[:, t * P:t * P + P], ident)
                        c_vt.up(ins)
                    col(2 * s + 1)
                    if s == 3:
                        sum_head_squares(0)
                        sum_head_squares(1)
                    if s == 4:
                        sum_head_squares(2)
                        sum_head_squares(3)
                    if s == 5:
                        sum_head_squares(4)
                        pe.wait_ge(sem("pool_w_landed"), 16 * (layer + 1))
                        pe.wait_ge(sem("head_variance_written"), layer + 1)
                        for g in range(4):
                            pe.wait_ge(sem("pool_diff_written"), 4 * layer + g + 1)
                            c_poolp.up(pe.matmul(banks[3 + g][:, :], pool_w_sb[:, g, :],
                                                 pool_u[:, g, PAD:PAD + TOKENS], start=True, stop=True))
                        spread_head(0)
                        spread_head(1)
                    if s == 6:
                        for ci in (0, 1):
                            swap_head(ci)
                        spread_head(2)
                        spread_head(3)
                    if s == 7:
                        swap_head(2)
                        swap_head(3)
                        spread_head(4)
                        swap_head(4)
                    if s >= 10:
                        values(2 * (s - 10))
                        values(2 * (s - 10) + 1)
                    if s >= 9:
                        turn(2 * (s - 9))
                        turn(2 * (s - 9) + 1)
                    if 8 <= s <= 11:
                        score(2 * (s - 8))
                        score(2 * (s - 8) + 1)
                values(6)
                values(7)

                order = (0, 1, 2, 3, 4, 5, 6, 7)
                for branch, (m_hi, m_lo) in enumerate(((y_hi, y_lo), (att_hi, att_lo))):
                    for n in order:
                        tile = tm + IN_TILES + 2 * branch + n // 4
                        if n % 4 == 0:
                            wait_tile(tile)
                        if branch == 0 and n == 0:
                            pe.wait_ge(sem("y_lo_written"), 4 * layer + 4)
                            pe.wait_ge(sem("column_read"), 26 * layer + 26)
                            pe.wait_ge(sem("probs_t_written"), 8 * layer + 8)
                        if branch == 0 and n == 3:
                            pe.wait_ge(sem("att_lo_written"), 8 * layer + 8)
                        if branch == 1:
                            pe.wait_ge(sem("pool_gated"), KB * layer + n + 1)
                        for r in range(4):
                            last = product(banks[n][:, :], tile % 2, 4 * r + n % 4, m_hi[:, r, :], m_lo[:, r, :],
                                           r == 0, r == 3)
                        (used if n % 4 == 3 else c_branch).up(last)
                for n in range(KB):
                    tile = tm + IN_TILES + 4 + n // 2
                    if n % 2 == 0:
                        wait_tile(tile)
                    for r in range(KB):
                        if n == 0:
                            pe.wait_ge(sem("mix_lo_written"), KB * layer + r + 1)
                        last = product(banks[n][:, :], tile % 2, 2 * r + n % 2, *mixed[r],
                                       r == 0, r == KB - 1)
                    (used if n % 2 else c_delta).up(last)


            def second_mixer():
                k = 6
                xu = KB * (k - 1)
                c_small = Count(pe, sem("gate_sums_done"))
                c_bc = Count(pe, sem("m_spread"))
                c_st = Count(pe, sem("ml_scores_done"))
                c_pv = Count(pe, sem("ml_values_done"))
                c_qs = Count(pe, sem("qk_squares_summed"))
                c_col2 = Count(pe, sem("column2_done"))
                c_vt2 = Count(pe, sem("values2_turned"))

                tile = IN2_AT
                wait_tile(tile)
                pe.wait_ge(sem("x_updated"), xu + 1)
                for n in range(KB):
                    pe.wait_ge(sem("h_lo_written"), KB * k + n + 1)
                    cols = slice(2 * n * P, 2 * n * P + 32)
                    o = banks[0][0:32, :]
                    pe.matmul(o, w_hi[:, tile % 2, cols], h_hi[:, n, :], start=(n == 0), stop=False)
                    pe.matmul(o, w_hi[:, tile % 2, cols], h_lo[:, n, :], start=False, stop=False)
                    last = pe.matmul(o, w_lo[:, tile % 2, cols], h_hi[:, n, :], start=False, stop=(n == KB - 1))
                    if n == KB - 1:
                        used.up(last)
                    pe.wait_ge(sem("squares_written"), KB * k + n + 1)
                    if n == 0:
                        pe.wait_ge(sem("x_updated"), xu + 2)
                    for t in range(TT):
                        ins = pe.matmul(banks[1][:, t:t + 1], sq[:, n % 2, t * P:t * P + P], ones[:, 0:1],
                                        start=(n == 0 and t == 0), stop=(n == KB - 1), skip_group_check=True)
                    c_stat.up(ins)
                pe.wait_ge(sem("x_updated"), xu + 8)
                spread_rstd(k, 7)
                pe.wait_ge(sem("gate_rows_written"), 1)
                for t in range(TT):
                    ins = pe.transpose(banks[0][:, 32 * t:32 * t + 32], tmp[0:32, t * P:t * P + P], ident[0:32, 0:32])
                c_small.up(ins)

                def columns2(s, halves=(0, 1)):
                    tile = IN2_AT + s
                    wait_tile(tile)
                    for half in halves:
                        if s == 1:
                            pe.wait_ge(sem("gates_read"), 1)
                        else:
                            pe.wait_ge(sem("column2_read"), 2 * (s - 1) + half - 1)
                        last = column((0, 2)[half], tile % 2, half)
                        (used if half else c_col2).up(last)

                def sums_of_gates():
                    pe.wait_ge(sem("logs_written"), 1)
                    for d in range(2):
                        tri = (upper, lower)[d]
                        for t in range(TT):
                            col = 8 * t + 4 * d
                            cols = slice(4 * d, 4 * d + 4)
                            pe.matmul(banks[3][:, col:col + 4], tri, decay[:, t, cols], start=True, stop=True)
                            pe.matmul(banks[3][:, 32 + col:36 + col], ones, decay[:, t, cols], start=True, stop=True)
                            before = list(range(t) if d == 0 else range(t + 1, TT))
                            for q in before:
                                pe.matmul(banks[3][:, 64 + col:68 + col], ones, logf[:, q, cols],
                                          start=(q == before[0]), stop=False)
                            ins = pe.matmul(banks[3][:, 64 + col:68 + col], tri, logf[:, t, cols],
                                            start=not before, stop=True)
                    c_small.up(ins)

                def rows_of_a(d):
                    if d == 0:
                        pe.wait_ge(sem("a_written"), 1)
                    for t in range(TT):
                        ins = pe.matmul(banks[4 + d][0:GH, t * P:t * P + P], a_col[:, t, 4 * d:4 * d + 4], ident,
                                        start=True, stop=True)
                    c_small.up(ins)

                def columns_of_m():
                    pe.wait_ge(sem("m_rows"), 2)
                    for d in range(2):
                        for t in range(TT):
                            ins = pe.matmul(banks[6][:, 8 * t + 4 * d:8 * t + 4 * d + 4],
                                            m_row[:, d, t * P:t * P + P], ident[0:GH, 0:GH], start=True, stop=True)
                    c_small.up(ins)

                def turn_values(n):
                    pe.wait_ge(sem("column2_read"), 2 * (5 + n))
                    for half in range(2):
                        for t in range(TT):
                            ins = pe.transpose(banks[(5, 7)[half]][:, t * P:t * P + P], sq[:, half, t * P:t * P + P],
                                               ident)
                        c_vt2.up(ins)

                def spread_m(u):
                    direction, h = unit_of(u)
                    if u == 0:
                        pe.wait_ge(sem("floor_args"), 1)
                        pe.wait_ge(sem("column2_read"), 12)
                    else:
                        pe.wait_ge(sem("p_args"), TT * u)
                    c_bc.up(pe.matmul(banks[1][:, :], ident[0:GH, h:h + 1].to_broadcast([GH, P]),
                                      m_row[:, direction, :], start=True, stop=True))

                def unit_scores(u, tiles=range(TT)):
                    direction, h = unit_of(u)
                    for a in tiles:
                        lo, up = span(direction, a)
                        if TT * u + a >= 2:
                            pe.wait_ge(sem("p_scored"), TT * u + a - 1)
                        c_st.up(pe.matmul(banks[3 + a % 2][:, lo:up], mk[:, h, a * P:a * P + P], mq[:, h, lo:up],
                                          start=True, stop=True))

                def unit_values(u):
                    direction, h = unit_of(u)
                    pe.wait_ge(sem("p_masked"), TT * u + TT)
                    if u >= 1:
                        pe.wait_ge(sem("h_written"), u)
                    for c in range(TT):
                        keys = range(0, c + 1) if direction == 0 else range(c, TT)
                        at = 256 * (c % 2)
                        for a in keys:
                            ins = pe.matmul(banks[5 + c // 2][:, at:at + P + 2], p_t[:, u % 2, a, c * P:c * P + P],
                                            mv[:, a, h, :], start=(a == keys[0]), stop=(a == keys[-1]))
                    c_pv.up(ins)

                def sum_squares(c):
                    pe.wait_ge(sem("qk_squares_written"), c + 1)
                    for t in range(TT):
                        ins = pe.matmul(banks[7][:, 8 * t + c:8 * t + c + 1], sq[:, c % 2, t * P:t * P + P],
                                        ones[:, 0:1], start=True, stop=True)
                    c_qs.up(ins)

                for s in range(1, 13):
                    if s >= 7:
                        spread_m(s - 7)
                        unit_scores(s - 7, (0, 1))
                        columns2(s, (0,))
                        if s == 7:
                            turn_values(1)
                        unit_scores(s - 7, (2, 3))
                        columns2(s, (1,))
                    elif s == 6:
                        columns2(s, (0,))
                        turn_values(0)
                        columns2(s, (1,))
                    else:
                        columns2(s)
                    if s == 1:
                        sums_of_gates()
                    if s == 3:
                        rows_of_a(0)
                        rows_of_a(1)
                    if s == 4:
                        columns_of_m()
                    if 8 <= s <= 11:
                        sum_squares(2 * (s - 8))
                        sum_squares(2 * (s - 8) + 1)
                    if s >= 8:
                        unit_values(s - 8)
                for u in (6, 7):
                    spread_m(u)
                    unit_scores(u)
                    unit_values(u - 1)
                unit_values(7)

                c_sp = Count(pe, sem("qk_rstd_spread"))
                c_rows = Count(pe, sem("rows_turned"))
                pe.wait_ge(sem("qk_rcol"), 1)
                for c in range(8):
                    bank = banks[c % 2]
                    if c >= 2:
                        pe.wait_ge(sem("qk_normed"), c - 1)
                    elif c == 0:
                        pe.wait_ge(sem("column2_read"), 24)
                    for t in range(TT):
                        ins = pe.matmul(bank[:, t * P:t * P + P], r3[:, 2, t, c:c + 1].to_broadcast([P, P]), ident,
                                        start=True, stop=True)
                    c_sp.up(ins)
                pe.wait_ge(sem("h_written"), 8)
                pe.wait_ge(sem("conv_activated"), 12)
                for n in range(8):
                    src, h = (gv, n) if n < 4 else (gk, n - 4)
                    if n >= 4:
                        pe.wait_ge(sem("qk_normed"), n + 1)
                    if n >= 2:
                        pe.wait_ge(sem("rows_written"), n - 1)
                    bank = banks[(2, 3)[n % 2]]
                    for t in range(TT):
                        ins = pe.transpose(bank[:, t * P:t * P + P], src[:, h, t * P:t * P + P], ident)
                    c_rows.up(ins)

                c_prep = Count(pe, sem("decay_spread"))
                c_kk = Count(pe, sem("keys_met"))
                c_turn2 = Count(pe, sem("a_turned"))
                c_ly = Count(pe, sem("level_y"))
                c_li = Count(pe, sem("level_inv"))
                c_lz = Count(pe, sem("level_inv_t"))
                c_ks = Count(pe, sem("state_read"))
                c_vn = Count(pe, sem("v_new_done"))
                c_o = Count(pe, sem("o_done"))
                c_s = Count(pe, sem("state_added"))
                pe.wait_ge(sem("rows_written"), 8)
                pe.wait_ge(sem("qk_normed"), 8)
                for pair in range(4):
                    items = (2 * pair, 2 * pair + 1)
                    for m in items:
                        d, c = item_of(m)
                        tok = slice(c * P, c * P + P)
                        b = 4 * (m % 2)
                        if m >= 2:
                            pe.wait_ge(sem("state_written"), 4 * (m - 1))
                            pe.wait_ge(sem("o_written"), m - 1)
                        for h in range(GH):
                            ins = pe.matmul(banks[b][:, h * P:h * P + P],
                                            decay[:, c, 4 * d + h:4 * d + h + 1].to_broadcast([P, P]),
                                            (upper, lower)[d], start=True, stop=True)
                        c_prep.up(ins)
                        for h in range(GH):
                            hs = slice(h * P, h * P + P)
                            pe.matmul(banks[b + 1][:, hs], beta[:, c, 4 * d + h:4 * d + h + 1].to_broadcast([P, P]),
                                      ident, start=True, stop=True)
                            pe.matmul(banks[b + 2][:, hs], gk[:, h, tok], gk[:, h, tok], start=True, stop=True)
                            ins = pe.matmul(banks[b + 3][:, hs], gk[:, h, tok], gq[:, h, tok], start=True, stop=True)
                        c_kk.up(ins)
                    for m in items:
                        b = 4 * (m % 2)
                        a_t = item_bufs[m % 2][0]
                        pe.wait_ge(sem("a_written2"), m + 1)
                        pe.wait_ge(sem("decay_exp"), 2 * m + 2)
                        for h in range(GH):
                            ins = pe.transpose(banks[b][:, h * P:h * P + P], a_t[:, h, :], ident)
                        c_turn2.up(ins)
                    for level in range(1, 7):
                        for m in items:
                            b = 4 * (m % 2)
                            b_t, inv = item_bufs[m % 2][2], item_bufs[m % 2][1]
                            pe.wait_ge(sem("level_masked"), level_index(pair, level, m) + 1)
                            for h in range(GH):
                                ins = pe.matmul(banks[b][:, h * P:h * P + P], b_t[:, h, :], inv[:, h, :],
                                                start=True, stop=True)
                            c_ly.up(ins)
                        if level == 1:
                            for m in items:
                                d, c = item_of(m)
                                pe.wait_ge(sem("inv_t_written"), inv_t_index(pair, 0, m) + 1)
                                for h in range(GH):
                                    ins = pe.matmul(banks[4 * (m % 2) + 3][:, h * P:h * P + P],
                                                    gk[:, h, c * P:c * P + P], state[:, d, h, :], start=True, stop=True)
                                c_ks.up(ins)
                        for m in items:
                            b = 4 * (m % 2)
                            _, inv, _, prod_y, inv_t, *_ = item_bufs[m % 2]
                            pe.wait_ge(sem("level_copied"), level_index(pair, level, m) + 1)
                            pe.wait_ge(sem("inv_t_written"), inv_t_index(pair, level - 1, m) + 1)
                            if level < 6:
                                for h in range(GH):
                                    ins = pe.matmul(banks[b + 1][:, h * P:h * P + P], inv_t[:, h, :], prod_y[:, h, :],
                                                    start=True, stop=True)
                                c_li.up(ins)
                            for h in range(GH):
                                ins = pe.matmul(banks[b + 2][:, h * P:h * P + P], prod_y[:, h, :], inv_t[:, h, :],
                                                start=True, stop=True)
                            c_lz.up(ins)
                    for m in items:
                        b = 4 * (m % 2)
                        inv_t = item_bufs[m % 2][4]
                        pe.wait_ge(sem("x_written2"), m + 1)
                        pe.wait_ge(sem("k_out_written"), m + 1)
                        pe.wait_ge(sem("inv_t_written"), inv_t_index(pair, 6, m) + 1)
                        for h in range(GH):
                            ins = pe.matmul(banks[b + 1][:, h * P:h * P + P], inv_t[:, h, :],
                                            sq[:, m % 2, h * P:h * P + P], start=True, stop=True)
                        c_vn.up(ins)
                    for m in items:
                        d, c = item_of(m)
                        b = 4 * (m % 2)
                        _, _, v_new, _, _, q_mask, q_in, k_out = item_bufs[m % 2]
                        pe.wait_ge(sem("v_new_written"), m + 1)
                        for h in range(GH):
                            ins = pe.matmul(banks[b + 3][:, h * P:h * P + P], k_out[:, h, :], v_new[:, h, :],
                                            start=True, stop=True)
                        c_s.up(ins)
                        for h in range(GH):
                            hs = slice(h * P, h * P + P)
                            pe.matmul(banks[b + 2][:, hs], q_in[:, h, :], state[:, d, h, :], start=True, stop=False)
                            ins = pe.matmul(banks[b + 2][:, hs], q_mask[:, h, :], v_new[:, h, :], start=False, stop=True)
                        c_o.up(ins)

                c_zc = Count(pe, sem("z_done"))
                c_yt = Count(pe, sem("y_turned"))
                for j in range(8):
                    tile = IN2_AT + 13 + j // 2
                    if j % 2 == 0:
                        wait_tile(tile)
                    if j == 0:
                        pe.wait_ge(sem("state_written"), 32)
                        pe.wait_ge(sem("o_written"), 8)
                    if j >= 2:
                        pe.wait_ge(sem("z_read"), j - 1)
                    last = column((0, 2)[j % 2], tile % 2, j % 2)
                    (used if j % 2 else c_zc).up(last)
                    pe.wait_ge(sem("heads_normed"), j // 4 + 1)
                    if j >= 2:
                        pe.wait_ge(sem("y2_written"), j - 1)
                    src = (o_gdn, h_ml)[j // 4]
                    for t in range(TT):
                        ins = pe.transpose(banks[(4, 5)[j % 2]][:, t * P:t * P + P], src[:, t, j % 4, :], ident)
                    c_yt.up(ins)
                for n in range(KB):
                    tile = OUT2_AT + n // 2
                    if n % 2 == 0:
                        wait_tile(tile)
                    if n == 0:
                        pe.wait_ge(sem("z_read"), 7)
                    for r in range(KB):
                        if n == 0:
                            pe.wait_ge(sem("y2_lo_written"), r + 1)
                        last = product(banks[n][:, :], tile % 2, 2 * r + n % 2, y2_hi[:, r, :], y2_lo[:, r, :],
                                       r == 0, r == KB - 1)
                    (used if n % 2 else c_delta).up(last)


            def experts():
                k = 7
                c_q = Count(pe, sem("query_done"))
                c_sc = Count(pe, sem("key_scores_done"))
                c_t = Count(pe, sem("chosen_turned"))
                c_quad = Count(pe, sem("quad_done"))
                c_sa = Count(pe, sem("s_ahead_done"))
                c_s = Count(pe, sem("s_done"))
                c_v = Count(pe, sem("v_done"))

                pe.wait_ge(sem("x_updated"), KB * (k - 1) + 1)
                c_q.up(first_column(k, WQ_AT, 0))
                pe.wait_ge(sem("x_updated"), KB * k)
                spread_rstd(k, 5)
                used.up(column(2, WQ_AT % 2, 1))
                for s in range(1, 8):
                    wait_tile(WQ_AT + s)
                    for half in range(2):
                        pe.wait_ge(sem("query_written"), 2 * s + half - 1)
                        (used if half else c_q).up(column((0, 2)[half], (WQ_AT + s) % 2, half))

                def key_scores(t):
                    for quarter in range(4):
                        n = 4 * t + quarter
                        if n >= 2:
                            pe.wait_ge(sem("key_scores_written"), n - 1)
                        for j in range(4):
                            hp = 4 * quarter + j
                            ins = pe.matmul(banks[3 + quarter % 2][:, j * P:j * P + P], qry[:, hp, t * P:t * P + P],
                                            keys_sb[:, hp, :], start=True, stop=True)
                        c_sc.up(ins)

                pe.wait_ge(sem("query_written"), 16)
                pe.wait_ge(sem("keys_landed"), 32)
                pe.wait_ge(sem("rstd_written"), k + 1)
                def ahead_row(n, e, part, i=None):
                    tile = TABLE_AT + n
                    if part == 0:
                        if e == 0:
                            wait_tile(tile, i)
                        if n > 0:
                            at = 2 * (n - 1) + e + 1
                            pe.wait_ge(sem("s_staged"), at if i is None else i * 4 + at)
                    for r in range(KB // 2 * part, KB // 2 * (part + 1)):
                        last = product(banks[e][:, :], tile % 2, KB * e + r, h_hi[:, r, :], h_lo[:, r, :],
                                       r == 0, r == KB - 1)
                    if part == 1:
                        (used if e else c_sa).up(last)

                def ahead(n, i=None):
                    for e in range(2):
                        for part in range(2):
                            ahead_row(n, e, part, i)

                key_scores(0)
                for t in range(TT):
                    n = CHOICE_TILES * t
                    if t + 1 < TT:
                        key_scores(t + 1)
                    ahead(n)
                    ahead(n + 1)
                    with pe.Fori(0, (CHOICE_TILES - 2) // 2) as i:
                        used.loop(i, 2)
                        c_sa.loop(i, 2)
                        ahead(n + 2, i)
                        ahead(n + 3, i)
                    used.end((CHOICE_TILES - 2) // 2)
                    c_sa.end((CHOICE_TILES - 2) // 2)
                    pe.wait_ge(sem("selected"), t + 1)
                    if t >= 1:
                        pe.wait_ge(sem("chosen_written"), t)
                    for n in range(3):
                        ins = pe.transpose(banks[5][:, n * P:n * P + P], sel[:, n].rearrange("p h k -> p (h k)"), ident)
                    c_t.up(ins)

                def quad(q, i=None):
                    pe.wait_ge(sem("hot_written"), q + 1 if i is None else i * PER_TRIP + (q + 1))
                    if q >= QUAD_BUFS:
                        at = q - QUAD_BUFS + 1
                        pe.wait_ge(sem("quad_stored"), at if i is None else i * PER_TRIP + at)
                    for n in range(4):
                        ins = pe.matmul(banks[quad_banks[q % 4]][:, n * P:n * P + P], hot[:, q % 4, n, 1, :],
                                        hot[:, q % 4, n, 0, :], start=True, stop=True)
                    c_quad.up(ins)

                PER_TRIP = 2 * CHUNK // 4

                def two_chunks(c, i=None):
                    for m in range(2):
                        for part in range(4):
                            for n in range(4):
                                quad(CHUNK // 4 * (c + m) + 4 * part + n, i)
                            ahead_row(CHOICE_TILES * TT + c + m, part // 2, part % 2, i)

                two_chunks(0)
                with pe.Fori(0, (CHUNKS - 2) // 2) as i:
                    c_quad.loop(i, PER_TRIP)
                    used.loop(i, 2)
                    c_sa.loop(i, 2)
                    two_chunks(2, i)
                for c in (c_quad, used, c_sa):
                    c.end((CHUNKS - 2) // 2)

                def s_products(g, i=None):
                    for e in range(EG):
                        tile = u_tile(g) + e // 2
                        if e % 2 == 0:
                            wait_tile(tile, i, 8)
                        if g > AHEAD:
                            at = EG * (g - 1) + e + 1
                            pe.wait_ge(sem("s_scaled_written"), at if i is None else i * (2 * EG) + at)
                        for n in range(KB):
                            last = product(banks[e][:, :], tile % 2, KB * (e % 2) + n, h_hi[:, n, :], h_lo[:, n, :],
                                           n == 0, n == KB - 1)
                        (used if e % 2 else c_s).up(last)

                def v_products(g, i=None, tiles=8):
                    pe.wait_ge(sem("weighed_lo_written"), EG * (g + 1) if i is None else i * (2 * EG) + EG * (g + 1))
                    for d in range(KB):
                        tile = v_tile(g) + d // 4
                        if d % 4 == 0:
                            wait_tile(tile, i, tiles)
                        if g > 0 or d >= 4 or i is not None:
                            at = KB * (7 + g) + d - 3
                            pe.wait_ge(sem("x_updated"), at if i is None else i * (2 * KB) + at)
                        for e in range(EG):
                            last = product(banks[4 + d % 4][:, :], tile % 2, 4 * e + d % 4, w_mix_hi[:, g % 2, e, :],
                                           w_mix_lo[:, g % 2, e, :], e == 0, e == EG - 1)
                        (used if d % 4 == 3 else c_v).up(last)

                for n in range(CHOICE_TILES * TT + CHUNKS, AHEAD_TILES):
                    ahead(n)

                pe.wait_ge(sem("quad_stored"), QUADS)
                pe.wait_ge(sem("s_staged"), 2 * AHEAD_TILES)
                v_products(0)
                v_products(1)
                with pe.Fori(0, (AHEAD - 4) // 2) as i:
                    used.loop(i, 4)
                    c_v.loop(i, 12)
                    v_products(2, i, 4)
                    v_products(3, i, 4)
                for c in (used, c_v):
                    c.end((AHEAD - 4) // 2)
                v_products(AHEAD - 2)
                s_products(AHEAD)
                v_products(AHEAD - 1)
                with pe.Fori(0, (GROUPS - AHEAD - 2) // 2) as i:
                    used.loop(i, 8)
                    c_s.loop(i, 4)
                    c_v.loop(i, 12)
                    for g in range(AHEAD, AHEAD + 2):
                        s_products(g + 1, i)
                        v_products(g, i)
                for c in (used, c_s, c_v):
                    c.end((GROUPS - AHEAD - 2) // 2)
                s_products(GROUPS - 1)
                v_products(GROUPS - 2)
                v_products(GROUPS - 1)

                k = 8
                for n in range(KB):
                    pe.wait_ge(sem("squares_written"), KB * k + n + 1)
                    for t in range(TT):
                        ins = pe.matmul(banks[1][:, t:t + 1], sq[:, n % 2, t * P:t * P + P], ones[:, 0:1],
                                        start=(n == 0 and t == 0), stop=(n == KB - 1), skip_group_check=True)
                    c_stat.up(ins)
                spread_rstd(k, 5)

            pe.wait_ge(sem("const_landed"), 16 * N_CONST)
            for layer in range(LAYERS):
                ffn(2 * layer)
                mix(layer)
                ffn(2 * layer + 1)
            second_mixer()
            experts()

        @block.vector
        def _(dve):
            local = Count(dve, sem("dve_local"))
            c_x = Count(dve, sem("x_updated"))
            c_hlo = Count(dve, sem("h_lo_written"))
            c_var = Count(dve, sem("variance_written"))
            c_rcol = Count(dve, sem("rcol_written"))
            c_rstd = Count(dve, sem("rstd_written"))
            c_gs = Count(dve, sem("gate_scaled"))
            c_us = Count(dve, sem("up_scaled"))
            c_prod = Count(dve, sem("prod_written"))
            c_alo = Count(dve, sem("act_lo_written"))
            c_read = Count(dve, sem("column_read"))
            c_diff = Count(dve, sem("pool_diff_written"))
            c_qvar = Count(dve, sem("head_variance_written"))
            c_qrcol = Count(dve, sem("head_rcol_written"))
            c_ylo = Count(dve, sem("y_lo_written"))
            c_normed = Count(dve, sem("head_normed"))
            c_swaps = Count(dve, sem("swap_scaled"))
            c_roped = Count(dve, sem("roped"))
            c_sread = Count(dve, sem("scores_read"))
            c_max = Count(dve, sem("max_written"))
            c_scaled = Count(dve, sem("probs_scaled"))
            c_attlo = Count(dve, sem("att_lo_written"))
            c_pg = Count(dve, sem("pool_gated"))
            c_mixed = Count(dve, sem("mixed"))
            c_mlo = Count(dve, sem("mix_lo_written"))

            def norm_operand(k):
                def low(n):
                    dve.wait_ge(sem("h_hi_written"), KB * k + n + 1)
                    c_hlo.up(dve.scalar_tensor_tensor(h_lo[:, n, :], x[:, n, :], gain[:, k, n:n + 1],
                                                        h_hi[:, n, :].bitcast(F32), ALU.mult, ALU.subtract))

                for n in range(KB):
                    if k > 0:
                        wait_delta(dve, k - 1, n)
                        scale = 1.0 if delta_signals(k - 1) == 4 else 0.5
                        c_x.up(dve.scalar_tensor_tensor(x[:, n, :], banks[n][:, :], scale, x[:, n, :],
                                                          ALU.mult, ALU.add))
                    elif n == 0:
                        dve.wait_ge(sem("x_landed"), 16)
                        dve.wait_ge(sem("const_landed"), 16 * N_CONST)
                    if n >= 1:
                        low(n - 1)
                low(KB - 1)
                dve.wait_ge(sem("squares_summed"), KB * (k + 1))
                c_var.step(dve.tensor_scalar(rcol[:, 0, :], banks[1][:, 0:TT], 1.0 / D, EPS, ALU.mult, ALU.add))
                dve.wait_ge(sem("deviation_written"), k + 1)
                c_rcol.step(dve.reciprocal(rcol[:, 2, :], rcol[:, 1, :]))
                dve.wait_ge(sem("rstd_spread"), k + 1)
                c_rstd.step(dve.tensor_copy(rstd[:, :], banks[7 if k in (1, 4, 6) else 5][:, :]))

            def ffn(f):
                t0, k = ffn_of(f)
                norm_operand(k)

                def step(s, i=None):
                    gate_bank, up_bank = ((0, 2), (3, 4))[s % 2]
                    at = s if i is None else i * 2 + s
                    dve.wait_ge(sem("gate_done"), at + (FB * f + 1))
                    c_gs.step(dve.tensor_tensor(gate_s[:, :], banks[gate_bank][:, :], rstd[:, :], ALU.mult))
                    dve.wait_ge(tile_used, at + (t0 + 1))
                    c_us.step(dve.tensor_tensor(up_s[:, :], banks[up_bank][:, :], rstd[:, :], ALU.mult))
                    dve.wait_ge(sem("silu_written"), at + (FB * f + 1))
                    c_prod.step(dve.tensor_tensor(prod[:, :], up_s[:, :], silu[:, :], ALU.mult))
                    dve.wait_ge(sem("act_hi_written"), at + (FB * f + 1))
                    c_alo.step(dve.tensor_tensor(act_lo[:, at, :], prod[:, :], act_hi[:, at, :].bitcast(F32),
                                                 ALU.subtract))

                step(0)
                step(1)
                loops = (c_gs, c_us, c_prod, c_alo)
                with dve.Fori(0, (FB - 2) // 2) as i:
                    for c in loops:
                        c.loop(i, 2)
                    for u in range(2):
                        step(2 + u, i)
                for c in loops:
                    c.end((FB - 2) // 2)

            def mix(layer):
                tm, k = mix_of(layer)
                norm_operand(k)
                gq = small_sb[:, layer, 0:1]
                gk = small_sb[:, layer, 1:2]
                sink = small_sb[:, layer, 6:14]

                def wait_col(c):
                    if c % 2 == 0:
                        dve.wait_ge(sem("column_done"), 13 * layer + c // 2 + 1)
                    else:
                        dve.wait_ge(tile_used, tm + c // 2 + 1)

                def read(c, dst):
                    wait_col(c)
                    c_read.step(dve.tensor_tensor(dst, banks[(0, 2)[c % 2]][:, :], rstd[:, :], ALU.mult))

                def gate_cols(s):
                    for c in (2 * s, 2 * s + 1):
                        read(c, gates[:, c - 10, :])

                def windows():
                    body = slice(PAD, PAD + TOKENS)
                    for g, w in enumerate(POOL_WINDOWS):
                        src, half, b = pool_u[:, g, :], 1, 0
                        while half < w:
                            local.step(dve.tensor_tensor(pool_s[:, b, body], src[:, body],
                                                         src[:, PAD - half:PAD - half + TOKENS], ALU.add))
                            src, b, half = pool_s[:, b, :], 1 - b, 2 * half
                        head = slice(PAD, 2 * PAD)
                        rest = slice(2 * PAD, PAD + TOKENS)
                        local.step(dve.tensor_tensor(src[:, head], src[:, head], invc[:, g, :], ALU.mult))
                        local.step(dve.tensor_tensor(pool_u[:, g, head], src[:, head], pool_u[:, g, head],
                                                     ALU.subtract))
                        c_diff.step(dve.scalar_tensor_tensor(pool_u[:, g, rest], src[:, rest], 1.0 / w,
                                                             pool_u[:, g, rest], ALU.mult, ALU.subtract))

                def normed(ci):
                    dve.wait_ge(sem("head_rstd_spread"), 5 * layer + ci + 1)
                    c_normed.step(dve.scalar_tensor_tensor(qk[:, ci, :], qk[:, ci, :], gk if ci == 4 else gq,
                                                           banks[4 + ci % 2][:, :], ALU.mult, ALU.mult))

                def roped(ci):
                    dve.wait_ge(sem("swapped"), 5 * layer + ci + 1)
                    c_swaps.step(dve.tensor_tensor(tmp[:, :], banks[(6, 3)[ci % 2]][:, :], rope_sb[:, 1, :],
                                                   ALU.mult))
                    local.step(dve.tensor_tensor(qk[:, ci, :], qk[:, ci, :], rope_sb[:, 0, :], ALU.mult))
                    c_roped.step(dve.tensor_tensor(qk[:, ci, :], qk[:, ci, :], tmp[:, :], ALU.add))

                def softmax_max(u):
                    n, hk = divmod(u, 2)
                    b, lo = u % 2, 0 if n else P
                    dve.wait_ge(sem("scores_done"), 8 * layer + u + 1)
                    if u >= 2:
                        dve.wait_ge(sem("probs_turned"), 8 * layer + u - 1)
                    for half in range(2):
                        bank = banks[3 + 2 * hk + half][:, :].rearrange("p (b k) -> p b k", b=2)[:, :, lo:]
                        c_sread.step(dve.scalar_tensor_tensor(
                            scores[b][:, half, :, lo:], bank, HD ** -0.5,
                            mask[:, None, lo:].to_broadcast([P, 2, 2 * P - lo]), ALU.mult, ALU.add))
                    s = soft[:, b]
                    sk = sink[:, 4 * hk:4 * hk + 4]
                    local.step(dve.tensor_reduce(s[:, 0, :].rearrange("p (a b) -> p a b", a=2),
                                                 scores[b][:, :, :, lo:], AX_X, ALU.max))
                    local.step(dve.tensor_tensor(s[:, 0, :], s[:, 0, :], sk, ALU.max))
                    local.step(dve.tensor_scalar(s[:, 1, :], s[:, 0, :], -1.0, None, ALU.mult))
                    c_max.step(dve.tensor_tensor(s[:, 2, :], sk, s[:, 0, :], ALU.subtract))

                def softmax_scale(u):
                    b, lo = u % 2, 0 if u >= 2 else P
                    s = soft[:, b]
                    dve.wait_ge(sem("exp_written"), 8 * layer + u + 1)
                    local.step(dve.tensor_tensor(s[:, 4, :], s[:, 3, :], s[:, 5, :], ALU.add))
                    local.step(dve.reciprocal(s[:, 4, :], s[:, 4, :]))
                    for g in range(GROUP):
                        p = scores[b][:, g // 2, g % 2, lo:]
                        ins = dve.tensor_scalar(p, p, s[:, 4, g:g + 1], None, ALU.mult)
                    c_scaled.step(ins)

                def att_low(u):
                    rows = slice(64 * (u % 2), 64 * (u % 2) + 64)
                    tok = slice(u // 2 * P, u // 2 * P + P)
                    dve.wait_ge(sem("att_hi_written"), 8 * layer + u + 1)
                    out_bank = banks[3 + 2 * (u % 2)][rows, :].rearrange("p (g q) -> p g q", g=4)
                    c_attlo.step(dve.tensor_tensor(att_lo[rows, :, tok], out_bank,
                                                   att_hi[rows, :, tok].bitcast(F32), ALU.subtract))

                local.step(dve.memset(pool_u[:, :, 0:PAD], 0.0))
                local.step(dve.memset(pool_s[:, :, 0:PAD], 0.0))
                for s in range(IN_TILES):
                    if s < 2:
                        read(2 * s, pool_u[:, 2 * s, PAD:PAD + TOKENS])
                        read(2 * s + 1, pool_u[:, 2 * s + 1, PAD:PAD + TOKENS])
                    elif s < 4:
                        read(2 * s, qk[:, 2 * s - 4, :])
                        read(2 * s + 1, qk[:, 2 * s - 3, :])
                    elif s == 4:
                        read(8, qk[:, 4, :])
                        read(9, tmp[:, :])
                    elif s == 5:
                        dve.wait_ge(sem("values_turned"), layer + 1)
                        local.step(dve.tensor_copy(v_tok[:, :, :], banks[7][:, :].rearrange("p (t n) -> p t n", t=TT)))
                        gate_cols(s)
                    else:
                        gate_cols(s)
                    if s == 3:
                        windows()
                    if s == 5:
                        dve.wait_ge(sem("head_squares_summed"), 5 * layer + 5)
                        c_qvar.step(dve.tensor_scalar(
                            rq[:, 0], banks[3][:, 0:10 * TT].rearrange("p (t c) -> p t c", t=TT),
                            1.0 / HD, EPS, ALU.mult, ALU.add))
                        dve.wait_ge(sem("head_deviation_written"), layer + 1)
                        c_qrcol.step(dve.reciprocal(rq[:, 2], rq[:, 1]))
                        for g in range(4):
                            dve.wait_ge(sem("y_hi_written"), 4 * layer + g + 1)
                            c_ylo.step(dve.scalar_tensor_tensor(
                                y_lo[:, g, :], banks[3 + g][:, :], small_sb[:, layer, 2 + g:3 + g],
                                y_hi[:, g, :].bitcast(F32), ALU.mult, ALU.subtract))
                        normed(0)
                        normed(1)
                    if s == 6:
                        roped(0)
                        roped(1)
                        normed(2)
                        normed(3)
                    if s == 7:
                        roped(2)
                        roped(3)
                        normed(4)
                        roped(4)
                    if s >= 10:
                        att_low(2 * (s - 10))
                        att_low(2 * (s - 10) + 1)
                    if 8 <= s <= 11:
                        for u in (2 * (s - 8), 2 * (s - 8) + 1):
                            softmax_max(u)
                        for u in (2 * (s - 8), 2 * (s - 8) + 1):
                            softmax_scale(u)
                att_low(6)
                att_low(7)
                for n in range(KB):
                    dve.wait_ge(sem("sigmoid_written"), 2 * KB * layer + n + 1)
                    if n % 4 == 3:
                        dve.wait_ge(tile_used, tm + IN_TILES + n // 4 + 1)
                    else:
                        dve.wait_ge(sem("branch_done"), 12 * layer + n - n // 4 + 1)
                    c_pg.step(dve.tensor_tensor(gates[:, n, :], gates[:, n, :], banks[n][:, :], ALU.mult))
                for n in range(KB):
                    dve.wait_ge(sem("sigmoid_written"), 2 * KB * layer + KB + n + 1)
                    if n % 4 == 3:
                        dve.wait_ge(tile_used, tm + IN_TILES + 2 + n // 4 + 1)
                    else:
                        dve.wait_ge(sem("branch_done"), 12 * layer + 6 + n - n // 4 + 1)
                    local.step(dve.tensor_tensor(gates[:, KB + n, :], gates[:, KB + n, :], banks[n][:, :], ALU.mult))
                    c_mixed.step(dve.tensor_tensor(gates[:, n, :], gates[:, n, :], gates[:, KB + n, :], ALU.add))
                    dve.wait_ge(sem("mix_hi_written"), KB * layer + n + 1)
                    c_mlo.step(dve.tensor_tensor(mixed[n][1], gates[:, n, :], mixed[n][0].bitcast(F32),
                                                 ALU.subtract))


            def second_mixer():
                k = 6
                norm_operand(k)
                bias = gbias[:, None, 0:32].to_broadcast([P, TT, 32])
                dve.wait_ge(tile_used, IN2_AT + 1)
                dve.tensor_copy(tmp[0:32, :], banks[0][0:32, :]).then_inc(sem("gate_rows_written"), 1)
                dve.wait_ge(sem("second_landed"), 64)
                dve.wait_ge(sem("gate_sums_done"), 1)
                for t in range(TT):
                    ins = dve.tensor_scalar(gt[:, t, :], banks[0][:, 32 * t:32 * t + 32], rcol[:, 2, t:t + 1], None,
                                            ALU.mult)
                local.step(ins)
                local.step(dve.tensor_tensor(gt[:, :, :], gt[:, :, :], bias, ALU.add))
                c_gr = Count(dve, sem("gates_read"))
                c_gr.step(dve.scalar_tensor_tensor(g_abs[:, :, :], gt[:, :, :], -1.0, gt[:, :, :], ALU.mult, ALU.min))
                dve.wait_ge(sem("gate_logs"), 4)
                local.step(dve.scalar_tensor_tensor(decay[:, :, :], gt[:, :, 0:8], 0.0, g_log[:, :, 0:8],
                                                    ALU.max, ALU.add))
                local.step(dve.scalar_tensor_tensor(decay[:, :, :], decay[:, :, :], -1.0,
                                                    gbias[:, None, 32:40].to_broadcast([P, TT, 8]), ALU.mult, ALU.mult))
                c_logs = Count(dve, sem("logs_written"))
                c_logs.step(dve.scalar_tensor_tensor(logf[:, :, :], gt[:, :, 24:32], 0.0, g_log[:, :, 24:32],
                                                     ALU.min, ALU.subtract))

                c_read2 = Count(dve, sem("column2_read"))

                def wait_col2(s, half):
                    if half == 0:
                        dve.wait_ge(sem("column2_done"), s)
                    else:
                        dve.wait_ge(tile_used, IN2_AT + s + 1)

                def read2(s, half, dst, scale=1.0):
                    wait_col2(s, half)
                    c_read2.step(dve.scalar_tensor_tensor(dst, banks[(0, 2)[half]][:, :], scale, rstd[:, :],
                                                          ALU.mult, ALU.mult))

                c_conv = Count(dve, sem("convolved"))
                c_args = Count(dve, sem("p_args"))
                c_sd = Count(dve, sem("p_scored"))
                c_pm = Count(dve, sem("p_masked"))
                c_h = Count(dve, sem("h_written"))

                def convolve(c):
                    s, half = 7 + c // 2, c % 2
                    read2(s, half, conv_in[:, c % 2, 2:2 + TOKENS])
                    dst = (gq, gk, gv)[c // 4][:, c % 4, :]
                    for tap in range(CONV):
                        src = conv_in[:, c % 2, tap:tap + TOKENS]
                        w = conv_sb[:, c, tap:tap + 1]
                        if tap == 0:
                            local.step(dve.tensor_scalar(dst, src, w, None, ALU.mult))
                        else:
                            ins = dve.scalar_tensor_tensor(dst, src, w, dst, ALU.mult, ALU.add)
                            (c_conv if tap == CONV - 1 else local).step(ins)

                def unit_args(u):
                    direction, h = unit_of(u)
                    p = p_t[:, u % 2]
                    dve.wait_ge(sem("m_spread"), u + 1)
                    if u >= 2:
                        dve.wait_ge(sem("ml_values_done"), u - 1)
                    for a in range(TT):
                        lo, up = span(direction, a)
                        c_args.up(dve.tensor_scalar(p[:, a, lo:up], banks[1][:, lo:up],
                                                    a_col[:, a, 4 * direction + h:4 * direction + h + 1], 0.0,
                                                    ALU.subtract, ALU.max))

                def unit_weights(u, tiles=range(TT)):
                    direction, h = unit_of(u)
                    p = p_t[:, u % 2]
                    for a in tiles:
                        lo, up = span(direction, a)
                        dve.wait_ge(sem("p_exp_written"), TT * u + a + 1)
                        dve.wait_ge(sem("ml_scores_done"), TT * u + a + 1)
                        c_sd.step(dve.tensor_tensor(p[:, a, lo:up], p[:, a, lo:up], banks[3 + a % 2][:, lo:up],
                                                    ALU.mult))
                        diagonal = p[:, a, a * P:a * P + P]
                        c_pm.step(dve.tensor_tensor(diagonal, diagonal, (upper, lower)[direction], ALU.mult))

                def unit_out(u):
                    direction, h = unit_of(u)
                    dve.wait_ge(sem("ml_values_done"), u + 1)
                    for half in range(2):
                        src = banks[5 + half][:, :].rearrange("p (c n) -> p c n", c=2)[:, :, P]
                        local.step(dve.tensor_copy(den[:, 0, 2 * half:2 * half + 2], src))
                    local.step(dve.scalar_tensor_tensor(den[:, 1, :], den[:, 0, :], -1.0, den[:, 0, :],
                                                        ALU.mult, ALU.max))
                    local.step(dve.tensor_tensor(den[:, 1, :], den[:, 1, :], floor[:, :, 4 * direction + h], ALU.max))
                    local.step(dve.reciprocal(den[:, 1, :], den[:, 1, :]))
                    for c in range(TT):
                        num = banks[5 + c // 2][:, 256 * (c % 2):256 * (c % 2) + P]
                        dst = h_ml[:, c, h, :]
                        if direction == 0:
                            ins = dve.tensor_scalar(dst, num, den[:, 1, c:c + 1], None, ALU.mult)
                        else:
                            ins = dve.scalar_tensor_tensor(dst, num, den[:, 1, c:c + 1], dst, ALU.mult, ALU.add)
                    c_h.step(ins)

                def keep_values(n):
                    for half in range(2):
                        dve.wait_ge(sem("values2_turned"), 2 * n + half + 1)
                        local.step(dve.tensor_copy(mv[:, :, 2 * n + half, 0:P],
                                                   banks[(5, 7)[half]][:, :].rearrange("p (t n) -> p t n", t=TT)))

                local.step(dve.memset(mv[:, :, :, P:P + 2], 1.0))
                local.step(dve.memset(conv_in[:, :, 0:2], 0.0))
                local.step(dve.memset(conv_in[:, :, 2 + TOKENS:], 0.0))
                for s in range(1, 13):
                    if s == 7:
                        dve.wait_ge(sem("gate_logs"), 8)
                    if s >= 7:
                        unit_args(s - 7)
                    for half in range(2):
                        if s - half == 6:
                            keep_values(s - 6)
                        if s >= 7:
                            unit_weights(s - 7, (2 * half, 2 * half + 1))
                        if s in (1, 2):
                            read2(s, half, mq[:, 2 * (s - 1) + half, :])
                        elif s in (3, 4):
                            read2(s, half, mk[:, 2 * (s - 3) + half, :], P ** -0.5)
                        elif s in (5, 6):
                            read2(s, half, sq[:, half, :])
                        else:
                            convolve(2 * (s - 7) + half)
                    if s == 1:
                        dve.wait_ge(sem("gate_sums_done"), 2)
                        local.step(dve.tensor_copy(sums[:, :, :, :],
                                                   banks[3][:, 0:96].rearrange("p (a t c) -> p a t c", a=3, t=TT)))
                        local.step(dve.tensor_tensor(a_col[:, :, :], gt[:, :, 16:24], sums[:, 2], ALU.subtract))
                        c_aw = Count(dve, sem("a_written"))
                        c_aw.step(dve.tensor_copy(floor[:, :, :], sums[:, 2]))
                        c_sw = Count(dve, sem("sums_written"))
                        c_sw.step(dve.tensor_tensor(e_out[:, :, :], sums[:, 1], sums[:, 0], ALU.subtract))
                    if s == 3:
                        c_mr = Count(dve, sem("m_rows"))
                        for d in range(2):
                            dve.wait_ge(sem("gate_sums_done"), 3 + d)
                            local.step(dve.tensor_copy(a_row[0:GH, :], banks[4 + d][0:GH, :]))
                            step = (1, -1)[d]
                            c_mr.step(dve.tensor_tensor_scan(m_row[:, d, ::step], a_row[0:GH, ::step],
                                                             a_row[0:GH, ::step], 0.0, ALU.max, ALU.max))
                    if s == 4:
                        dve.wait_ge(sem("gate_sums_done"), 5)
                        c_fa = Count(dve, sem("floor_args"))
                        c_fa.step(dve.tensor_tensor(floor[:, :, :], floor[:, :, :],
                                                    banks[6][:, 0:32].rearrange("p (t c) -> p t c", t=TT), ALU.add))
                        dve.wait_ge(sem("gate_logs"), 7)
                        local.step(dve.scalar_tensor_tensor(e_in[:, :, :], e_in[:, :, :], -1.0, beta[:, :, :],
                                                            ALU.mult, ALU.mult))
                    if s >= 8:
                        unit_out(s - 8)
                for u in (6, 7):
                    unit_args(u)
                    unit_weights(u)
                    unit_out(u - 1)
                unit_out(7)

                dve.wait_ge(sem("qk_squares_summed"), 8)
                dve.wait_ge(sem("conv_activated"), 12)
                dve.tensor_scalar(r3[:, 0], banks[7][:, 0:32].rearrange("p (t c) -> p t c", t=TT), EPS,
                                  None, ALU.add).then_inc(sem("qk_variance"), 1)
                dve.wait_ge(sem("qk_deviation"), 1)
                local.step(dve.reciprocal(r3[:, 2], r3[:, 1]))
                c_rc = Count(dve, sem("qk_rcol"))
                c_rc.step(dve.tensor_scalar(r3[:, 2, :, 0:4], r3[:, 2, :, 0:4], P ** -0.5, None, ALU.mult))
                c_nm = Count(dve, sem("qk_normed"))
                c_rw = Count(dve, sem("rows_written"))

                def norm_col(c):
                    dve.wait_ge(sem("qk_rstd_spread"), c + 1)
                    g = (gq, gk)[c // 4][:, c % 4, :]
                    c_nm.step(dve.tensor_tensor(g, g, banks[c % 2][:, :], ALU.mult))

                for c in range(8):
                    norm_col(c)
                for n in range(8):
                    dve.wait_ge(sem("rows_turned"), n + 1)
                    dst = (v_rows, k_rows)[n // 4][:, :, n % 4, :]
                    c_rw.step(dve.tensor_copy(dst, banks[(2, 3)[n % 2]][:, :].rearrange("p (t n) -> p t n", t=TT)))

                c_da = Count(dve, sem("decay_args"))
                c_aw2 = Count(dve, sem("a_written2"))
                c_lm = Count(dve, sem("level_masked"))
                c_it = Count(dve, sem("inv_t_written"))
                c_ko = Count(dve, sem("k_out_written"))
                c_xw = Count(dve, sem("x_written2"))
                c_sw2 = Count(dve, sem("state_written"))
                c_ow = Count(dve, sem("o_written"))
                local.step(dve.memset(state[:, :, :, :], 0.0))

                def bank4(n):
                    return banks[n][:, :].rearrange("p (h t) -> p h t", h=GH)

                def over_heads(m2):
                    return m2[:, None, :].to_broadcast([P, GH, P])

                for pair in range(4):
                    items = (2 * pair, 2 * pair + 1)
                    for m in items:
                        d, c = item_of(m)
                        b = 4 * (m % 2)
                        arg = item_bufs[m % 2][3]
                        dve.wait_ge(sem("decay_spread"), m + 1)
                        for h in range(GH):
                            ins = dve.tensor_scalar(arg[:, h, :], banks[b][:, h * P:h * P + P],
                                                    sums[:, 0, c, 4 * d + h:4 * d + h + 1], 0.0, ALU.subtract, ALU.min)
                        c_da.step(ins)
                    for m in items:
                        d, c = item_of(m)
                        b = 4 * (m % 2)
                        tok = slice(c * P, c * P + P)
                        a_t, inv, b_t, e, inv_t, q_mask, q_in, k_out = item_bufs[m % 2]
                        dve.wait_ge(sem("decay_exp"), 2 * m + 2)
                        dve.wait_ge(sem("keys_met"), m + 1)
                        local.step(dve.tensor_tensor(a_t[:, :, :], e[:, :, :], bank4(b + 1), ALU.mult))
                        local.step(dve.tensor_tensor(a_t[:, :, :], a_t[:, :, :], bank4(b + 2), ALU.mult))
                        c_aw2.step(dve.tensor_tensor(a_t[:, :, :], a_t[:, :, :], over_heads(masks2[:, d, :]), ALU.mult))

                    def mask_level(m, level):
                        a_t, _, b_t = item_bufs[m % 2][:3]
                        c_lm.step(dve.tensor_tensor(b_t[:, :, :], a_t[:, :, :], over_heads(masks2[:, 2 + level, :]),
                                                    ALU.mult))

                    for m in items:
                        d, c = item_of(m)
                        b = 4 * (m % 2)
                        tok = slice(c * P, c * P + P)
                        a_t, inv, b_t, e, inv_t, q_mask, q_in, k_out = item_bufs[m % 2]
                        local.step(dve.tensor_tensor(q_in[:, :, :], gq[:, :, tok], b_t[:, :, :], ALU.mult))
                        local.step(dve.tensor_tensor(inv_t[:, :, :], a_t[:, :, :], over_heads(masks2[:, 2, :]), ALU.mult))
                        local.step(dve.tensor_tensor(inv_t[:, :, :], over_heads(ident), inv_t[:, :, :], ALU.subtract))
                        dve.wait_ge(sem("a_turned"), m + 1)
                        local.step(dve.tensor_tensor(inv[:, :, :], bank4(b), over_heads(masks2[:, 2, :]), ALU.mult))
                        local.step(dve.tensor_tensor(inv[:, :, :], over_heads(ident), inv[:, :, :], ALU.subtract))
                        mask_level(m, 1)
                        c_it.step(dve.tensor_tensor(q_mask[:, :, :], e[:, :, :], bank4(b + 3), ALU.mult))
                    for m in items:
                        q_mask = item_bufs[m % 2][5]
                        local.step(dve.tensor_tensor(q_mask[:, :, :], q_mask[:, :, :],
                                                     over_heads((upper, lower)[m % 2]), ALU.mult))
                    for level in range(1, 7):
                        for m in items:
                            b = 4 * (m % 2)
                            inv, inv_t = item_bufs[m % 2][1], item_bufs[m % 2][4]
                            if level < 6:
                                dve.wait_ge(sem("level_inv"), 10 * pair + 2 * (level - 1) + m % 2 + 1)
                                local.step(dve.tensor_tensor(inv[:, :, :], inv[:, :, :], bank4(b + 1), ALU.subtract))
                                mask_level(m, level + 1)
                            dve.wait_ge(sem("level_inv_t"), level_index(pair, level, m) + 1)
                            update = dve.tensor_tensor(inv_t[:, :, :], inv_t[:, :, :], bank4(b + 2), ALU.subtract)
                            c_it.step(update)
                        if level == 2:
                            for m in items:
                                d, c = item_of(m)
                                k_out = item_bufs[m % 2][7]
                                for h in range(GH):
                                    at = slice(4 * d + h, 4 * d + h + 1)
                                    dve.tensor_scalar(sq[:, m % 2, h * P:h * P + P], v_rows[:, c, h, :],
                                                      beta[:, c, at], None, ALU.mult)
                                    ins = dve.tensor_scalar(k_out[:, h, :], k_rows[:, c, h, :], e_out[:, c, at], None,
                                                            ALU.mult)
                                c_ko.step(ins)
                        if level == 3:
                            for m in items:
                                d, c = item_of(m)
                                dve.wait_ge(sem("state_read"), m + 1)
                                for h in range(GH):
                                    hs = slice(h * P, h * P + P)
                                    ins = dve.scalar_tensor_tensor(sq[:, m % 2, hs], banks[4 * (m % 2) + 3][:, hs],
                                                                   e_in[:, c, 4 * d + h:4 * d + h + 1],
                                                                   sq[:, m % 2, hs], ALU.mult, ALU.add)
                                c_xw.step(ins)
                    for m in items:
                        d, c = item_of(m)
                        b = 4 * (m % 2)
                        dve.wait_ge(sem("o_done"), m + 1)
                        for h in range(GH):
                            c_sw2.step(dve.scalar_tensor_tensor(state[:, d, h, :], state[:, d, h, :],
                                                           e_all[:, c, 4 * d + h:4 * d + h + 1],
                                                           banks[b + 3][:, h * P:h * P + P], ALU.mult, ALU.add))
                        if pair < 2:
                            c_ow.step(dve.tensor_copy(o_gdn[:, c, :, :], bank4(b + 2)))
                        else:
                            c_ow.step(dve.tensor_tensor(o_gdn[:, c, :, :], o_gdn[:, c, :, :], bank4(b + 2), ALU.add))

                dve.wait_ge(sem("act_local"), 2 * TT * GH)
                c_ov = Count(dve, sem("out_variance"))
                c_ov.step(dve.tensor_scalar(rn[:, 0, :], rn[:, 0, :], 1.0 / P, EPS, ALU.mult, ALU.add))
                dve.wait_ge(sem("out_deviation"), 1)
                local.step(dve.reciprocal(rn[:, 2, :], rn[:, 1, :]))
                c_hn = Count(dve, sem("heads_normed"))

                def norm_heads(which):
                    buf = (o_gdn, h_ml)[which]
                    for t in range(TT):
                        for h in range(GH):
                            at = 16 * which + 4 * t + h
                            ins = dve.tensor_scalar(buf[:, t, h, :], buf[:, t, h, :], rn[:, 2, at:at + 1], None, ALU.mult)
                    c_hn.step(ins)

                norm_heads(0)
                c_zr = Count(dve, sem("z_read"))
                c_y2 = Count(dve, sem("y2_written"))
                c_y2lo = Count(dve, sem("y2_lo_written"))
                for j in range(8):
                    zb = (gq, gk)[j % 2]
                    if j % 2:
                        dve.wait_ge(tile_used, IN2_AT + 13 + j // 2 + 1)
                    else:
                        dve.wait_ge(sem("z_done"), j // 2 + 1)
                    c_zr.step(dve.tensor_tensor(zb[:, 0, :], banks[(0, 2)[j % 2]][:, :], rstd[:, :], ALU.mult))
                    dve.wait_ge(sem("z_activated"), j + 1)
                    dve.wait_ge(sem("y_turned"), j + 1)
                    c_y2.step(dve.scalar_tensor_tensor(zb[:, 1, :], banks[(4, 5)[j % 2]][:, :], head_gain[:, j:j + 1],
                                                       zb[:, 0, :], ALU.mult, ALU.mult))
                    if j == 1:
                        norm_heads(1)
                    dve.wait_ge(sem("y2_hi_written"), j + 1)
                    c_y2lo.step(dve.tensor_tensor(y2_lo[:, j, :], zb[:, 1, :], y2_hi[:, j, :].bitcast(F32),
                                                  ALU.subtract))


            def experts():
                norm_operand(7)
                c_top = Count(dve, sem("top_keys_written"))
                c_args = Count(dve, sem("gate_args_written"))
                c_sel = Count(dve, sem("selected"))
                c_cho = Count(dve, sem("chosen_written"))
                c_hot = Count(dve, sem("hot_written"))
                c_ss = Count(dve, sem("s_scaled_written"))
                c_wg = Count(dve, sem("weighed_written"))
                c_wl = Count(dve, sem("weighed_lo_written"))
                c_res = Count(dve, sem("result_written"))
                LOWEST = -3.0e38

                def top16(values, rest, best_v, best_i):
                    for n in range(len(values)):
                        ins = dve.max(best_v[:, n, 0:8], values[n])
                    local.step(ins)
                    for n in range(len(values)):
                        ins = dve.max_index(best_i[:, n, 0:8], best_v[:, n, 0:8], values[n])
                    local.step(ins)
                    for n in range(len(values)):
                        ins = dve.match_replace(rest[n], best_v[:, n, 0:8], values[n], LOWEST)
                    local.step(ins)
                    for n in range(len(values)):
                        ins = dve.max(best_v[:, n, 8:16], rest[n])
                    local.step(ins)
                    for n in range(len(values)):
                        ins = dve.max_index(best_i[:, n, 8:16], best_v[:, n, 8:16], rest[n])
                    local.step(ins)

                def keep_chosen(t):
                    dve.wait_ge(sem("chosen_turned"), t + 1)
                    c_cho.step(dve.tensor_copy(chosen[:, :, t * P:t * P + P],
                                               banks[5][:, 0:3 * P].rearrange("p (a b) -> p a b", a=3)))

                for t in range(TT):
                    dve.wait_ge(sem("key_scores_written"), 4 * t + 4)
                    top16([sc[:, t % 2, n, :] for n in range(16)], [sc[:, t % 2, n, :] for n in range(16)], top, top_at)
                    c_top.step(dve.tensor_copy(top_key[:, :, :], top_at[:, :, :]))
                    by_half = top[:, :, :].rearrange("p (h a) k -> p h a k", a=2)
                    local.step(dve.tensor_tensor(cand[:, :, :, :],
                                                 by_half[:, :, 0, :, None].to_broadcast([P, PEER_HEADS, TOPK, TOPK]),
                                                 by_half[:, :, 1, None, :].to_broadcast([P, PEER_HEADS, TOPK, TOPK]),
                                                 ALU.add))
                    flat = lambda buf, h: buf[:, h].rearrange("p a b -> p (a b)")
                    top16([flat(cand, h) for h in range(PEER_HEADS)], [flat(cand_rest, h) for h in range(PEER_HEADS)],
                          best, best_at)
                    if t >= 1:
                        keep_chosen(t - 1)
                    c_args.step(dve.tensor_tensor(sel[:, 2], best[:, :, :],
                                                  best[:, :, 0:1].to_broadcast([P, PEER_HEADS, TOPK]), ALU.subtract))
                    local.step(dve.tensor_scalar(pair_at[:, 0], best_at[:, :, :], 4, None, ALU.logical_shift_right))
                    local.step(dve.tensor_scalar(pair_at[:, 1], best_at[:, :, :], 15, None, ALU.bitwise_and))
                    local.step(dve.tensor_copy(pair_f[:, :, :, :], pair_at[:, :, :, :]))
                    keys_by_half = top_key[:, :, :].rearrange("p (h a) k -> p h a k", a=2)
                    for half in range(2):
                        shape = [P, PEER_HEADS, TOPK, TOPK]
                        local.step(dve.tensor_tensor(picks[:, :, :, :],
                                                     pair_f[:, half, :, :, None].to_broadcast(shape),
                                                     numbers[:, None, None, 0:TOPK].to_broadcast(shape), ALU.is_equal))
                        local.step(dve.tensor_tensor(picks[:, :, :, :], picks[:, :, :, :],
                                                     keys_by_half[:, :, half, None, :].to_broadcast(shape), ALU.mult))
                        local.step(dve.tensor_reduce(sel[:, half], picks[:, :, :, :], AX_X, ALU.add))
                    dve.wait_ge(sem("gates_exp"), t + 1)
                    local.step(dve.tensor_reduce(gate_sum[:, 0, :], sel[:, 2], AX_X, ALU.add))
                    local.step(dve.reciprocal(gate_sum[:, 1, :], gate_sum[:, 0, :]))
                    c_sel.step(dve.tensor_tensor(sel[:, 2], sel[:, 2],
                                                 gate_sum[:, 1, :, None].to_broadcast([P, PEER_HEADS, TOPK]), ALU.mult))
                keep_chosen(TT - 1)

                def hots(q, i=None):
                    if q >= QUAD_BUFS:
                        dve.wait_ge(sem("quad_done"), i * QUAD_BUFS + (q - QUAD_BUFS + 1))
                    for n in range(4):
                        at = slice(4 * q + n, 4 * q + n + 1) if i is None else bass.ds(dve.snap(i * (4 * QUAD_BUFS) + (4 * q + n)), 1)
                        dve.tensor_scalar(hot[:, q % 4, n, 0, :], numbers[:, :], chosen[:, 0, at], chosen[:, 2, at],
                                          ALU.is_equal, ALU.mult)
                    four = slice(4 * q, 4 * q + 4) if i is None else bass.ds(dve.snap(i * (4 * QUAD_BUFS) + 4 * q), 4)
                    c_hot.up(dve.tensor_tensor(hot[:, q % 4, :, 1, :], numbers[:, None, :].to_broadcast([P, 4, P]),
                                               chosen[:, 1, four, None].to_broadcast([P, 4, P]), ALU.is_equal))

                for q in range(QUAD_BUFS):
                    hots(q)
                with dve.Fori(0, QUADS // QUAD_BUFS - 1) as i:
                    c_hot.loop(i, QUAD_BUFS)
                    for q in range(QUAD_BUFS, 2 * QUAD_BUFS):
                        hots(q, i)
                c_hot.end(QUADS // QUAD_BUFS - 1)

                chunked = lambda ap: ap.rearrange("p (c t) -> p c t", c=CHUNKS)

                def mix_group(g, i=None, rows=range(EG), fill=lambda: None):
                    slot = g % 2
                    there = 16 * (g // 2 + 1)
                    for e in rows:
                        if g < AHEAD:
                            if e == 0:
                                dve.wait_ge(sem(f"s_landed{slot}"), there if i is None else i * 16 + there)
                            source = s_in[:, slot, e, :]
                        else:
                            source = banks[e][:, :]
                            if e % 2:
                                tile = u_tile(g) + e // 2
                                dve.wait_ge(tile_used, tile + 1 if i is None else i * 8 + (tile + 1))
                            else:
                                at = 2 * (g - AHEAD) + e // 2 + 1
                                dve.wait_ge(sem("s_done"), at if i is None else i * 4 + at)
                        c_ss.step(dve.tensor_tensor(s_scaled[:, :], source, rstd[:, :], ALU.mult))
                        at = EG * g + e + 1
                        if e == 0:
                            dve.wait_ge(sem(f"gates_landed{slot}"), there if i is None else i * 16 + there)
                        fill()
                        dve.wait_ge(sem("gelu_written"), at if i is None else i * (2 * EG) + at)
                        c_wg.step(dve.tensor_tensor(chunked(weighed[:, :]), chunked(gelu[:, :]),
                                                    g_in[:, slot, :, e, :], ALU.mult))
                        fill()
                        dve.wait_ge(sem("weighed_hi_written"), at if i is None else i * (2 * EG) + at)
                        c_wl.step(dve.tensor_tensor(w_mix_lo[:, slot, e, :], weighed[:, :],
                                                    w_mix_hi[:, slot, e, :].bitcast(F32), ALU.subtract))

                def add_group(g, i=None, tiles=8, blocks=range(KB)):
                    for d in blocks:
                        if d % 4 == 3:
                            tile = v_tile(g) + d // 4
                            dve.wait_ge(tile_used, tile + 1 if i is None else i * tiles + (tile + 1))
                        else:
                            at = 6 * g + d - d // 4 + 1
                            dve.wait_ge(sem("v_done"), at if i is None else i * 12 + at)
                        c_x.up(dve.tensor_tensor(x[:, d, :], x[:, d, :], banks[4 + d % 4][:, :], ALU.add))

                def early_group(g, i=None):
                    sums = iter(range(KB))
                    add = lambda: add_group(g - 1, i, 4, (next(sums),))
                    mix_group(g, i, (0, 1))
                    add()
                    mix_group(g, i, (2, 3), add)
                    for d in sums:
                        add_group(g - 1, i, 4, (d,))

                def late_group(g, i=None):
                    mix_group(g, i)
                    add_group(g - 1, i)

                def looped(trips, g, body):
                    with dve.Fori(0, trips) as i:
                        for c in (c_ss, c_wg, c_wl):
                            c.loop(i, 2 * EG)
                        c_x.loop(i, 2 * KB)
                        body(g, i)
                        body(g + 1, i)
                    for c in (c_ss, c_wg, c_wl, c_x):
                        c.end(trips)

                for b in range(2):
                    dve.wait_ge(sem(f"gates_stored{b}"), 16 * CHUNKS // 2)
                mix_group(0)
                looped((AHEAD - 2) // 2, 1, early_group)
                early_group(AHEAD - 1)
                late_group(AHEAD)
                looped((GROUPS - AHEAD - 2) // 2, AHEAD + 1, late_group)
                late_group(GROUPS - 1)
                add_group(GROUPS - 1)

                k = 8
                dve.wait_ge(sem("squares_summed"), KB * (k + 1))
                c_var.step(dve.tensor_scalar(rcol[:, 0, :], banks[1][:, 0:TT], 1.0 / D, EPS, ALU.mult, ALU.add))
                dve.wait_ge(sem("deviation_written"), k + 1)
                c_rcol.step(dve.reciprocal(rcol[:, 2, :], rcol[:, 1, :]))
                dve.wait_ge(sem("rstd_spread"), k + 1)
                for n in range(KB):
                    c_res.up(dve.scalar_tensor_tensor(x[:, n, :], x[:, n, :], gain[:, k, n:n + 1], banks[5][:, :],
                                                      ALU.mult, ALU.mult))

            for layer in range(LAYERS):
                ffn(2 * layer)
                mix(layer)
                ffn(2 * layer + 1)
            second_mixer()
            experts()


def constants():
    i = np.arange(P)
    c = np.zeros((P, 7 * P + 66), np.float32)
    c[:, 0:P] = np.eye(P)
    for m in range(P):
        d = m % HD
        if d < ROT:
            partner = m - d + (d + ROT // 2) % ROT
            c[partner, P + m] = 1.0
    c[:, 2 * P:3 * P] = i[:, None] <= i[None, :]
    c[:, 3 * P:4 * P] = i[:, None] >= i[None, :]
    c[:, 4 * P:5 * P] = 1.0
    diff = i[:, None] + P - np.arange(2 * P)[None, :]
    c[:, 5 * P:7 * P] = np.where((diff >= 0) & (diff < P), 0.0, -1e30)
    for g, w in enumerate(POOL_WINDOWS):
        c[:, 7 * P + 16 * g:7 * P + 16 * g + 16] = 1.0 / np.minimum(np.arange(PAD) + 1, w)
    c[:, 7 * P + 64] = i < HD
    c[:, 7 * P + 65] = i >= HD
    half = ROT // 2
    inv_freq = THETA ** (-np.arange(0, ROT, 2, dtype=np.float32) / np.float32(ROT))
    ang = (np.arange(TOKENS, dtype=np.float32)[:, None] * inv_freq[None, :].astype(np.float32))
    rope = np.zeros((P, 2, TOKENS), np.float32)
    rope[:, 0] = 1.0
    for m in range(P):
        d = m % HD
        if d < ROT:
            rope[m, 0] = np.cos(ang[:, d % half])
            rope[m, 1] = np.sin(ang[:, d % half]) * (-1.0 if d < half else 1.0)
    return c, rope


def pair_tiles(w):
    return w.reshape(KB, P, -1, 2, P).transpose(2, 1, 0, 3, 4).reshape(-1, P, TILE * P)


def lay_out(a):
    tiles = []

    def ffn(gu, down):
        tiles.append(gu.reshape(KB, P, 2, FB, P).transpose(3, 1, 0, 2, 4).reshape(FB, P, TILE * P))
        tiles.append(down.reshape(FB // 2, 2, P, KB, P).transpose(0, 2, 1, 3, 4).reshape(-1, P, TILE * P))

    def branch(w):
        tiles.append(w.reshape(4, P, 2, 4, P).transpose(2, 1, 0, 3, 4).reshape(2, P, TILE * P))

    for l in range(LAYERS):
        ffn(a["w_ffn1_gu"][l], a["w_ffn1_down"][l])
        w = a["w_in"][l]
        q = w[:, 512:1024].reshape(D, KV_HEADS, GROUP, HD).transpose(0, 2, 1, 3).reshape(D, 512)
        tiles.append(pair_tiles(np.concatenate([w[:, :512], q, w[:, 1024:]], axis=1)))
        branch(a["w_pool_branch"][l])
        branch(a["w_attn_branch"][l].reshape(KV_HEADS, GROUP, HD, D).transpose(1, 0, 2, 3).reshape(512, D))
        tiles.append(pair_tiles(a["w_out"][l]))
        ffn(a["w_ffn2_gu"][l], a["w_ffn2_down"][l])

    columns = lambda g: g.reshape(KB, P).T
    gains = np.stack([columns(g) for g in (
        a["ln_ffn1"][0], a["ln_mix"][0], a["ln_ffn2"][0], a["ln_ffn1"][1], a["ln_mix"][1],
        a["ln_ffn2"][1], a["norm1_g_2"][0], a["norm2_g_2"][0], a["normf_g_2"])], axis=1)
    small = np.zeros((P, LAYERS, 14), np.float32)
    for l in range(LAYERS):
        small[:, l, 0] = np.concatenate([a["q_norm"][l]] * 2)
        small[:, l, 1] = np.concatenate([a["k_norm"][l]] * 2)
        small[:, l, 2:6] = a["pool_scale"][l].reshape(4, P).T
        small[:, l, 6:14] = a["sinks"][l][None, :]
    w = a["w_in_2"][0]
    at = np.cumsum((0, 512, 512, 512, 512, 8, 8, 512, 512, 512, 512, 8, 8))
    cut = {name: w[:, at[n]:at[n + 1]] for n, name in enumerate("gq gk gv gz ga gb mq mk mv mo mi mf".split())}
    tiles.append(pair_tiles(np.concatenate(
        [cut["ga"], cut["gb"], cut["mi"], cut["mf"], np.zeros((D, 2 * P - 32), np.float32)]
        + [cut[n] for n in "mq mk mv gq gk gv gz mo".split()], axis=1)))
    tiles.append(pair_tiles(a["w_out_2"][0]))
    tiles.append(pair_tiles(a["peer_wq_2"][0]))
    u = a["peer_u_2"][0].reshape(GROUPS, 2, 2, P, KB, P).transpose(0, 1, 5, 2, 4, 3).reshape(GROUPS, 2, P, TILE * P)
    v = a["peer_v_2"][0].reshape(GROUPS, EG, P, 2, 4, P).transpose(0, 3, 2, 1, 4, 5).reshape(GROUPS, 2, P, TILE * P)
    order = [u[g] for g in range(AHEAD)] + [v[g] for g in range(AHEAD - 1)]
    for g in range(AHEAD, GROUPS):
        order += [u[g], v[g - 1]]
    tiles += order + [v[GROUPS - 1]]
    second = np.zeros((P, 108), np.float32)
    second[:, 0:8] = a["gdn_dt_bias_2"][0].reshape(1, 8)
    second[:, 16:24] = a["mlstm_i_bias_2"][0].reshape(1, 8)
    second[:, 24:32] = a["mlstm_f_bias_2"][0].reshape(1, 8)
    second[:, 32:40] = a["gdn_a_log_2"][0].reshape(1, 8)
    second[:, 40:100] = a["conv_w_2"][0].reshape(12, P, CONV).transpose(1, 0, 2).reshape(P, 60)
    second[:, 100:104] = a["gdn_norm_g_2"][0][:, None]
    second[:, 104:108] = a["mlstm_norm_g_2"][0].reshape(GH, P).T
    consts, rope = constants()
    i = np.arange(P)
    level_masks = np.zeros((P, 10, P), np.float32)
    level_masks[:, 9] = i[None, :]
    level_masks[:, 0] = i[:, None] < i[None, :]
    level_masks[:, 1] = i[:, None] > i[None, :]
    for b in range(7):
        level_masks[:, 2 + b] = ((i[:, None] >> (b + 1) == i[None, :] >> (b + 1))
                                 & (i[:, None] >> b != i[None, :] >> b))
    return dict(
        second=second, level_masks=level_masks,
        keys=a["peer_keys_2"][0].transpose(3, 0, 1, 2).reshape(P, 16, P),
        x_in=a["x"][0].T.reshape(KB, P, TOKENS).transpose(1, 0, 2),
        weights=np.concatenate(tiles), gains=gains, small=small,
        pool_w=a["pool_w"].transpose(0, 2, 1, 3), consts=consts, rope=rope)


def kernel(**inputs):
    import concourse.bacc as bacc
    from concourse.bass_utils import run_bass_kernel_spmd

    arrays = {name: np.ascontiguousarray(a) for name, a in
              lay_out({name: np.asarray(a) for name, a in inputs.items()}).items()}
    nc = bacc.Bacc("TRN2", target_bir_lowering=False, num_devices=1)
    args = {name: nc.dram_tensor(name, a.shape, mybir.dt.from_np(a.dtype), kind="ExternalInput").ap()
            for name, a in arrays.items()}
    out = nc.dram_tensor("out", [P, KB, TOKENS], F32, kind="ExternalOutput").ap()
    build(nc, out=out, **args)
    r = run_bass_kernel_spmd(nc, [arrays], core_ids=[0])
    return np.ascontiguousarray(r.results[0]["out"].transpose(2, 1, 0).reshape(1, TOKENS, D))
```
